# Optimizing a Trainium2 kernel written in Bass

```python
import math
import jax
import jax.numpy as jnp
from jax import lax
import numpy as np
import jax, jax.numpy as jnp

D_MODEL = 1024
BATCH = 1
SEQ = 256
DEPTH = 1

MOBA_HEADS = 8
MOBA_HEAD_DIM = 64
MOBA_BLOCK = 256
MOBA_TOPK = 3
MOBA_Q_CHUNK = 64
RG_WIDTH = D_MODEL
RG_BLOCKS = 16
RG_BLOCK_DIM = RG_WIDTH // RG_BLOCKS
RG_CONV = 4
RG_C = 8.0
RG_A_MIN = 0.9
RG_A_MAX = 0.999
DIFF_HEADS = 4
DIFF_HEAD_DIM = 64
DIFF_Q_BLOCK = 128
D_FF = 2816
FFN_CONV = 3
N_BRANCHES = 3
RMS_EPS = 1e-6

MOBA_WIDTH = MOBA_HEADS * MOBA_HEAD_DIM
DIFF_QK_WIDTH = DIFF_HEADS * 2 * DIFF_HEAD_DIM
DIFF_V_WIDTH = DIFF_HEADS * 2 * DIFF_HEAD_DIM
IN_WIDTHS = (MOBA_WIDTH, MOBA_WIDTH, MOBA_WIDTH, DIFF_QK_WIDTH, DIFF_QK_WIDTH, DIFF_V_WIDTH, RG_WIDTH, RG_WIDTH, N_BRANCHES * D_MODEL)
IN_COLS = sum(IN_WIDTHS)


def rms_norm(x, g):
    xf = x.astype(jnp.float32)
    y = xf * lax.rsqrt(jnp.mean(xf * xf, axis=-1, keepdims=True) + RMS_EPS)
    return (y * g.astype(jnp.float32)).astype(x.dtype)

def alibi_slopes(n):
    return 2.0 ** (-8.0 * jnp.arange(1, n + 1, dtype=jnp.float32) / n)

def causal_dwconv(x, w, b):
    k_w = w.shape[0]
    s = x.shape[1]
    xp = jnp.pad(x, ((0, 0), (k_w - 1, 0), (0, 0)))
    y = b
    for j in range(k_w):
        y = y + w[j] * xp[:, j:j + s]
    return y

def split_offsets():
    return np.cumsum(np.array(IN_WIDTHS[:-1])).tolist()

def moba_attention(q, k, v):
    B, S, H, D = q.shape
    nb = -(-S // MOBA_BLOCK)
    s_pad = nb * MOBA_BLOCK
    pad = ((0, 0), (0, s_pad - S), (0, 0), (0, 0))
    q, k, v = [jnp.pad(t, pad).transpose(0, 2, 1, 3) for t in (q, k, v)]
    kb = k.reshape(B, H, nb, MOBA_BLOCK, D)
    vb = v.reshape(B, H, nb, MOBA_BLOCK, D)
    slopes = alibi_slopes(H)[None, :, None, None]
    scale = D ** -0.5
    kmean = jnp.mean(kb.astype(jnp.float32), axis=3)
    gate = jnp.einsum('bhsd,bhnd->bhsn', q.astype(jnp.float32), kmean)
    q_blk = jnp.arange(s_pad) // MOBA_BLOCK
    past = jnp.arange(nb)[None, :] < q_blk[:, None]
    gate = jnp.where(past, gate, -jnp.inf)
    n_sel = min(MOBA_TOPK, nb)
    _, sel = lax.top_k(gate, n_sel)
    bi = jnp.arange(B)[:, None, None, None]
    hi = jnp.arange(H)[None, :, None, None]
    n_chunks = s_pad // MOBA_Q_CHUNK

    def chunk(c):
        q0 = c * MOBA_Q_CHUNK
        blk = q0 // MOBA_BLOCK
        qc = lax.dynamic_slice_in_dim(q, q0, MOBA_Q_CHUNK, axis=2)
        selc = lax.dynamic_slice_in_dim(sel, q0, MOBA_Q_CHUNK, axis=2)
        qpos = q0 + jnp.arange(MOBA_Q_CHUNK)
        k_own = lax.dynamic_index_in_dim(kb, blk, axis=2, keepdims=False)
        v_own = lax.dynamic_index_in_dim(vb, blk, axis=2, keepdims=False)
        kpos_own = blk * MOBA_BLOCK + jnp.arange(MOBA_BLOCK)
        dist_own = (qpos[:, None] - kpos_own[None, :]).astype(jnp.float32)
        l_own = jnp.einsum('bhqd,bhkd->bhqk', qc, k_own).astype(jnp.float32) * scale - slopes * dist_own
        l_own = jnp.where(dist_own >= 0, l_own, -jnp.inf)
        k_sel = kb[bi, hi, selc]
        v_sel = vb[bi, hi, selc]
        kpos_sel = selc[..., None] * MOBA_BLOCK + jnp.arange(MOBA_BLOCK)
        dist_sel = (qpos[None, None, :, None, None] - kpos_sel).astype(jnp.float32)
        l_sel = jnp.einsum('bhqd,bhqnkd->bhqnk', qc, k_sel).astype(jnp.float32) * scale - slopes[..., None] * dist_sel
        valid = (selc < blk)[..., None]
        l_sel = jnp.where(valid, l_sel, -jnp.inf)
        n_keys = n_sel * MOBA_BLOCK
        logits = jnp.concatenate([l_sel.reshape(B, H, MOBA_Q_CHUNK, n_keys), l_own], axis=-1)
        p = jax.nn.softmax(logits, axis=-1).astype(v.dtype)
        p_sel = p[..., :n_keys].reshape(B, H, MOBA_Q_CHUNK, n_sel, MOBA_BLOCK)
        p_own = p[..., n_keys:]
        return (jnp.einsum('bhqnk,bhqnkd->bhqd', p_sel, v_sel)
                + jnp.einsum('bhqk,bhkd->bhqd', p_own, v_own))

    out = lax.map(chunk, jnp.arange(n_chunks))
    out = out.transpose(1, 0, 3, 2, 4).reshape(B, s_pad, H, D)
    return out[:, :S]

def diff_attention(q, k, v, lam, lam_init, subln_g):
    B, S, H, _, Dh = q.shape
    q = q.transpose(0, 2, 3, 1, 4)
    k = k.transpose(0, 2, 3, 1, 4)
    v = v.transpose(0, 2, 1, 3)
    slopes = alibi_slopes(H)[None, :, None, None, None]
    scale = Dh ** -0.5
    kpos = jnp.arange(S)
    n_blocks = S // DIFF_Q_BLOCK

    def block(c):
        q0 = c * DIFF_Q_BLOCK
        qc = lax.dynamic_slice_in_dim(q, q0, DIFF_Q_BLOCK, axis=3)
        qpos = q0 + jnp.arange(DIFF_Q_BLOCK)
        dist = (qpos[:, None] - kpos[None, :]).astype(jnp.float32)
        logits = jnp.einsum('bhmqd,bhmkd->bhmqk', qc, k).astype(jnp.float32) * scale - slopes * dist
        logits = jnp.where(dist >= 0, logits, -jnp.inf)
        p = jax.nn.softmax(logits, axis=-1)
        w = p[:, :, 0] - lam * p[:, :, 1]
        return jnp.einsum('bhqk,bhkd->bhqd', w.astype(v.dtype), v)

    out = lax.map(block, jnp.arange(n_blocks))
    out = out.transpose(1, 0, 3, 2, 4).reshape(B, S, H, 2 * Dh)
    out = rms_norm(out, subln_g) * (1.0 - lam_init)
    return out.reshape(B, S, H * 2 * Dh)

def rg_lru(x, w_a, b_a, w_x, b_x, lam):
    B, S, C = x.shape
    xb = x.reshape(B, S, RG_BLOCKS, RG_BLOCK_DIM)
    r = jax.nn.sigmoid(jnp.einsum('bsnc,ncd->bsnd', xb, w_a).reshape(B, S, C) + b_a)
    i = jax.nn.sigmoid(jnp.einsum('bsnc,ncd->bsnd', xb, w_x).reshape(B, S, C) + b_x)
    log_a = -RG_C * r.astype(jnp.float32) * jax.nn.softplus(-lam.astype(jnp.float32))
    a = jnp.exp(log_a)
    mult = jnp.sqrt(-jnp.expm1(2.0 * log_a))
    b = mult * (i * x).astype(jnp.float32)

    def combine(left, right):
        a1, b1 = left
        a2, b2 = right
        return a1 * a2, a2 * b1 + b2

    _, h = lax.associative_scan(combine, (a, b), axis=1)
    return h.astype(x.dtype)

def first_inputs(seed: int = 0) -> dict:
    key = jax.random.key(seed)
    ks = jax.random.split(key, 26)
    f32 = jnp.float32
    L = DEPTH

    def nrm(k, shape, scale):
        return jax.random.normal(k, shape, f32) * scale

    def gain(k, shape):
        return 1.0 + nrm(k, shape, 0.01)

    a_c = jax.random.uniform(ks[10], (L, RG_WIDTH), f32, RG_A_MIN, RG_A_MAX)
    a0 = a_c ** (1.0 / RG_C)
    return {
        'x': nrm(ks[0], (BATCH, SEQ, D_MODEL), 1.0),
        'norm_mix_g': gain(ks[1], (L, D_MODEL)),
        'w_in': nrm(ks[2], (L, D_MODEL, IN_COLS), D_MODEL ** -0.5),
        'b_gate': nrm(ks[3], (L, N_BRANCHES * D_MODEL), 0.01),
        'rg_conv_w': nrm(ks[4], (L, RG_CONV, RG_WIDTH), RG_CONV ** -0.5),
        'rg_conv_b': nrm(ks[5], (L, RG_WIDTH), 0.01),
        'rg_w_a': nrm(ks[6], (L, RG_BLOCKS, RG_BLOCK_DIM, RG_BLOCK_DIM), RG_BLOCK_DIM ** -0.5),
        'rg_b_a': nrm(ks[7], (L, RG_WIDTH), 0.01),
        'rg_w_x': nrm(ks[8], (L, RG_BLOCKS, RG_BLOCK_DIM, RG_BLOCK_DIM), RG_BLOCK_DIM ** -0.5),
        'rg_b_x': nrm(ks[9], (L, RG_WIDTH), 0.01),
        'rg_lambda': jnp.log(a0) - jnp.log1p(-a0),
        'diff_lq1': nrm(ks[11], (L, DIFF_HEAD_DIM), 0.1),
        'diff_lk1': nrm(ks[12], (L, DIFF_HEAD_DIM), 0.1),
        'diff_lq2': nrm(ks[13], (L, DIFF_HEAD_DIM), 0.1),
        'diff_lk2': nrm(ks[14], (L, DIFF_HEAD_DIM), 0.1),
        'diff_subln_g': gain(ks[15], (L, 2 * DIFF_HEAD_DIM)),
        'w_branch_a': nrm(ks[16], (L, MOBA_WIDTH, D_MODEL), MOBA_WIDTH ** -0.5),
        'w_branch_b': nrm(ks[17], (L, RG_WIDTH, D_MODEL), RG_WIDTH ** -0.5),
        'w_branch_c': nrm(ks[18], (L, DIFF_V_WIDTH, D_MODEL), DIFF_V_WIDTH ** -0.5),
        'w_out': nrm(ks[19], (L, D_MODEL, D_MODEL), D_MODEL ** -0.5),
        'norm_ffn_g': gain(ks[20], (L, D_MODEL)),
        'ffn_up': nrm(ks[21], (L, D_MODEL, 2 * D_FF), D_MODEL ** -0.5),
        'ffn_conv_w': nrm(ks[22], (L, FFN_CONV, 2 * D_FF), FFN_CONV ** -0.5),
        'ffn_conv_b': nrm(ks[23], (L, 2 * D_FF), 0.01),
        'ffn_down': nrm(ks[24], (L, D_FF, D_MODEL), D_FF ** -0.5),
        'final_norm_g': gain(ks[25], (D_MODEL,)),
    }

def first_block(x, norm_mix_g, w_in, b_gate, rg_conv_w, rg_conv_b, rg_w_a, rg_b_a, rg_w_x, rg_b_x,
              rg_lambda, diff_lq1, diff_lk1, diff_lq2, diff_lk2, diff_subln_g, w_branch_a, w_branch_b,
              w_branch_c, w_out, norm_ffn_g, ffn_up, ffn_conv_w, ffn_conv_b, ffn_down, final_norm_g):
    B, S = x.shape[0], x.shape[1]
    offs = split_offsets()
    for l in range(DEPTH):
        h = rms_norm(x, norm_mix_g[l])
        proj = h @ w_in[l]
        qa, ka, va, qc, kc, vc, rx, rgate, gates = jnp.split(proj, offs, axis=-1)
        ya = moba_attention(qa.reshape(B, S, MOBA_HEADS, MOBA_HEAD_DIM),
                            ka.reshape(B, S, MOBA_HEADS, MOBA_HEAD_DIM),
                            va.reshape(B, S, MOBA_HEADS, MOBA_HEAD_DIM)).reshape(B, S, MOBA_WIDTH)
        xr = causal_dwconv(rx, rg_conv_w[l], rg_conv_b[l])
        yb = rg_lru(xr, rg_w_a[l], rg_b_a[l], rg_w_x[l], rg_b_x[l], rg_lambda[l]) * jax.nn.gelu(rgate)
        lam_init = 0.8 - 0.6 * math.exp(-0.3 * l)
        lam = (jnp.exp(jnp.sum(diff_lq1[l].astype(jnp.float32) * diff_lk1[l].astype(jnp.float32)))
               - jnp.exp(jnp.sum(diff_lq2[l].astype(jnp.float32) * diff_lk2[l].astype(jnp.float32)))
               + lam_init)
        yc = diff_attention(qc.reshape(B, S, DIFF_HEADS, 2, DIFF_HEAD_DIM),
                            kc.reshape(B, S, DIFF_HEADS, 2, DIFF_HEAD_DIM),
                            vc.reshape(B, S, DIFF_HEADS, 2 * DIFF_HEAD_DIM),
                            lam, lam_init, diff_subln_g[l])
        g = jax.nn.sigmoid(gates + b_gate[l]).reshape(B, S, N_BRANCHES, D_MODEL)
        merged = (g[:, :, 0] * (ya @ w_branch_a[l])
                  + g[:, :, 1] * (yb @ w_branch_b[l])
                  + g[:, :, 2] * (yc @ w_branch_c[l]))
        x = x + merged @ w_out[l]
        h = rms_norm(x, norm_ffn_g[l])
        u = causal_dwconv(h @ ffn_up[l], ffn_conv_w[l], ffn_conv_b[l])
        u_gate, u_val = jnp.split(u, 2, axis=-1)
        x = x + (jax.nn.gelu(u_gate) * u_val) @ ffn_down[l]
    return rms_norm(x, final_norm_g)


_first_inputs = first_inputs


def first_inputs(seed=0):
    import zlib

    import numpy as np

    out = dict(_first_inputs(seed))
    spreads = {}
    factors = {'norm_mix_g': 6.101,
     'b_gate': 25.959,
     'rg_conv_b': 3.952,
     'rg_b_a': 41.249,
     'rg_b_x': 34.099,
     'diff_lk2': 3.38,
     'diff_subln_g': 64.0,
     'norm_ffn_g': 34.906,
     'ffn_conv_b': 33.875,
     'final_norm_g': 31.228,
     'diff_lk1': 2.838}
    for name, (base, spread) in spreads.items():
        noise = np.random.default_rng([zlib.crc32(name.encode()), seed]).standard_normal(out[name].shape)
        drawn = base * np.exp(spread * noise) if base else spread * noise
        out[name] = jnp.asarray(drawn.astype(out[name].dtype))
    for name, factor in factors.items():
        out[name] = (out[name] * factor).astype(out[name].dtype)
    return out


_narrow_inputs = first_inputs


def first_inputs(seed=0):

    out = dict(_narrow_inputs(seed))
    wider = {'rg_conv_b': 4.18,
     'diff_subln_g': 4.82,
     'norm_ffn_g': 4.72,
     'ffn_conv_b': 4.69,
     'final_norm_g': 6.31}
    for name, times in wider.items():
        mean = out[name].mean()
        out[name] = (mean + times * (out[name] - mean)).astype(out[name].dtype)
    return out


DEPTH_2 = 2

POOL_WINDOWS = (2, 4, 8, 16)
N_POOL_GROUPS = 4
POOL_GROUP_DIM = D_MODEL // 16
POOL_WIDTH = N_POOL_GROUPS * POOL_GROUP_DIM
HEAD_DIM = 64
N_Q_HEADS = D_MODEL // 128
N_KV_HEADS = 2
GROUP = N_Q_HEADS // N_KV_HEADS
Q_WIDTH = N_Q_HEADS * HEAD_DIM
KV_WIDTH = N_KV_HEADS * HEAD_DIM
WINDOW = 128
ROT_DIM = HEAD_DIM // 4
ROPE_THETA = 500000.0
CONV_WIDTH = D_MODEL // 4
CONV_K = 3
IN_WIDTH = POOL_WIDTH + Q_WIDTH + 2 * KV_WIDTH + 3 * CONV_WIDTH + N_BRANCHES * D_MODEL
D_FF_2 = ((8 * D_MODEL // 3 + 127) // 128) * 128
FFN_K = 3
ALPHA = (2 * DEPTH_2) ** 0.25
BETA = (8 * DEPTH_2) ** -0.25
LN_EPS = 1e-5
MASK_VALUE = -1e30


def _split_points(sizes):
    pts, acc = [], 0
    for s in sizes[:-1]:
        acc += s
        pts.append(acc)
    return pts

def layer_norm(x, g, b):
    xf = x.astype(jnp.float32)
    mu = jnp.mean(xf, axis=-1, keepdims=True)
    var = jnp.mean(jnp.square(xf - mu), axis=-1, keepdims=True)
    y = (xf - mu) * lax.rsqrt(var + LN_EPS)
    return (y * g.astype(jnp.float32) + b.astype(jnp.float32)).astype(x.dtype)

def causal_dwconv_2(u, w):
    K = w.shape[0]
    S = u.shape[1]
    up = jnp.pad(u, ((0, 0), (K - 1, 0), (0, 0)))
    y = up[:, 0:S] * w[0]
    for k in range(1, K):
        y = y + up[:, k:k + S] * w[k]
    return y

def rope_tables(positions):
    inv_freq = ROPE_THETA ** (-jnp.arange(0, ROT_DIM, 2, dtype=jnp.float32) / ROT_DIM)
    ang = positions.astype(jnp.float32)[..., None] * inv_freq
    return jnp.cos(ang), jnp.sin(ang)

def apply_partial_rope(t, cos, sin):
    tf = t.astype(jnp.float32)
    half = ROT_DIM // 2
    x1, x2, rest = tf[..., :half], tf[..., half:ROT_DIM], tf[..., ROT_DIM:]
    c, s = cos[:, :, None, :], sin[:, :, None, :]
    out = jnp.concatenate([x1 * c - x2 * s, x2 * c + x1 * s, rest], axis=-1)
    return out.astype(t.dtype)

def multiscale_pool_mixer(u, w_pool, pool_scale):
    B, S, _ = u.shape
    ug = u.reshape(B, S, N_POOL_GROUPS, POOL_GROUP_DIM).astype(jnp.float32)
    csum = jnp.cumsum(ug, axis=1)
    t = jnp.arange(S)
    outs = []
    for g, w in enumerate(POOL_WINDOWS):
        c = csum[:, :, g]
        c_lag = jnp.pad(c[:, :S - w], ((0, 0), (w, 0), (0, 0)))
        count = jnp.minimum(t + 1, w).astype(jnp.float32)[None, :, None]
        outs.append((c - c_lag) / count - ug[:, :, g])
    pooled = jnp.stack(outs, axis=2).astype(u.dtype)
    mixed = jnp.einsum('bsgc,gcd->bsgd', pooled, w_pool)
    return mixed.reshape(B, S, POOL_WIDTH) * pool_scale

def sliding_window_gqa_sinks(q, k, v, sinks):
    B, S, _, D = q.shape
    nb = S // WINDOW
    qb = q.reshape(B, nb, WINDOW, N_KV_HEADS, GROUP, D)
    kb = k.reshape(B, nb, WINDOW, N_KV_HEADS, D)
    vb = v.reshape(B, nb, WINDOW, N_KV_HEADS, D)
    pad = ((0, 0), (1, 0), (0, 0), (0, 0), (0, 0))
    kcat = jnp.concatenate([jnp.pad(kb[:, :-1], pad), kb], axis=2)
    vcat = jnp.concatenate([jnp.pad(vb[:, :-1], pad), vb], axis=2)
    scores = jnp.einsum('bnqhgd,bnkhd->bnhgqk', qb, kcat).astype(jnp.float32)
    scores = scores * (HEAD_DIM ** -0.5)
    i = jnp.arange(WINDOW)[:, None]
    j = jnp.arange(2 * WINDOW)[None, :]
    band = (j > i) & (j <= i + WINDOW)
    blk = jnp.arange(nb)[:, None, None]
    valid = band[None] & ((blk > 0) | (j[None] >= WINDOW))
    scores = jnp.where(valid[None, :, None, None], scores, MASK_VALUE)
    sink = jnp.broadcast_to(
        sinks.astype(jnp.float32).reshape(1, 1, N_KV_HEADS, GROUP, 1, 1),
        scores.shape[:-1] + (1,))
    probs = jax.nn.softmax(jnp.concatenate([scores, sink], axis=-1), axis=-1)[..., :-1]
    out = jnp.einsum('bnhgqk,bnkhd->bnqhgd', probs.astype(v.dtype), vcat)
    return out.reshape(B, S, N_Q_HEADS * D)

def short_gated_conv(xc, gate_b, gate_c, conv_w):
    return gate_b * causal_dwconv_2(gate_c * xc, conv_w)

def hybrid_layer(x, cos, sin, w_in, w_pool, pool_scale, attn_sinks, conv_w,
                 w_branch_a, w_branch_b, w_branch_c, w_o, ln1_g, ln1_b,
                 w_up, ffn_conv_w, w_down, ln2_g, ln2_b):
    B, S, _ = x.shape
    proj = jnp.einsum('bsd,de->bse', x, w_in)
    sizes = [POOL_WIDTH, Q_WIDTH, KV_WIDTH, KV_WIDTH,
             CONV_WIDTH, CONV_WIDTH, CONV_WIDTH, N_BRANCHES * D_MODEL]
    u_pool, q, k, v, xc, gate_b, gate_c, gate_logits = jnp.split(
        proj, _split_points(sizes), axis=-1)
    o_a = multiscale_pool_mixer(u_pool, w_pool, pool_scale)
    q = apply_partial_rope(q.reshape(B, S, N_Q_HEADS, HEAD_DIM), cos, sin)
    k = apply_partial_rope(k.reshape(B, S, N_KV_HEADS, HEAD_DIM), cos, sin)
    v = v.reshape(B, S, N_KV_HEADS, HEAD_DIM)
    o_b = sliding_window_gqa_sinks(q, k, v, attn_sinks)
    o_c = short_gated_conv(xc, gate_b, gate_c, conv_w)
    gates = jax.nn.sigmoid(gate_logits).reshape(B, S, N_BRANCHES, D_MODEL)
    merged = (gates[:, :, 0] * jnp.einsum('bsc,cd->bsd', o_a, w_branch_a)
              + gates[:, :, 1] * jnp.einsum('bsc,cd->bsd', o_b, w_branch_b)
              + gates[:, :, 2] * jnp.einsum('bsc,cd->bsd', o_c, w_branch_c))
    mix = jnp.einsum('bsd,de->bse', merged, w_o)
    x = layer_norm(ALPHA * x + mix, ln1_g, ln1_b)
    up = causal_dwconv_2(jnp.einsum('bsd,df->bsf', x, w_up), ffn_conv_w)
    a, b = jnp.split(up, 2, axis=-1)
    ffn = jnp.einsum('bsf,fd->bsd', jax.nn.silu(a) * b, w_down)
    return layer_norm(ALPHA * x + ffn, ln2_g, ln2_b)

def second_inputs(seed: int = 0) -> dict:
    key = jax.random.key(seed)
    ks = jax.random.split(key, 20)
    nrm = lambda k, shape, scale: jax.random.normal(k, shape, jnp.float32) * scale
    x = nrm(ks[0], (BATCH, SEQ, D_MODEL), 1.0)
    offset = jax.random.randint(ks[1], (BATCH, 1), 0, 1024, dtype=jnp.int32)
    positions = offset + jnp.arange(SEQ, dtype=jnp.int32)[None, :]
    return {
        "x": x,
        "positions": positions,
        "w_in": nrm(ks[2], (DEPTH_2, D_MODEL, IN_WIDTH), D_MODEL ** -0.5),
        "w_pool": nrm(ks[3], (DEPTH_2, N_POOL_GROUPS, POOL_GROUP_DIM, POOL_GROUP_DIM), POOL_GROUP_DIM ** -0.5),
        "pool_scale": 1.0 + nrm(ks[4], (DEPTH_2, POOL_WIDTH), 0.1),
        "attn_sinks": nrm(ks[5], (DEPTH_2, N_Q_HEADS), 0.5),
        "conv_w": nrm(ks[6], (DEPTH_2, CONV_K, CONV_WIDTH), CONV_K ** -0.5),
        "w_branch_a": nrm(ks[7], (DEPTH_2, POOL_WIDTH, D_MODEL), POOL_WIDTH ** -0.5),
        "w_branch_b": nrm(ks[8], (DEPTH_2, Q_WIDTH, D_MODEL), Q_WIDTH ** -0.5),
        "w_branch_c": nrm(ks[9], (DEPTH_2, CONV_WIDTH, D_MODEL), CONV_WIDTH ** -0.5),
        "w_o": nrm(ks[10], (DEPTH_2, D_MODEL, D_MODEL), BETA * D_MODEL ** -0.5),
        "ln1_g": 1.0 + nrm(ks[11], (DEPTH_2, D_MODEL), 0.02),
        "ln1_b": nrm(ks[12], (DEPTH_2, D_MODEL), 0.02),
        "w_up": nrm(ks[13], (DEPTH_2, D_MODEL, 2 * D_FF_2), D_MODEL ** -0.5),
        "ffn_conv_w": nrm(ks[14], (DEPTH_2, FFN_K, 2 * D_FF_2), FFN_K ** -0.5),
        "w_down": nrm(ks[15], (DEPTH_2, D_FF_2, D_MODEL), BETA * D_FF_2 ** -0.5),
        "ln2_g": 1.0 + nrm(ks[16], (DEPTH_2, D_MODEL), 0.02),
        "ln2_b": nrm(ks[17], (DEPTH_2, D_MODEL), 0.02),
    }

def second_block(x, positions, w_in, w_pool, pool_scale, attn_sinks, conv_w,
              w_branch_a, w_branch_b, w_branch_c, w_o, ln1_g, ln1_b,
              w_up, ffn_conv_w, w_down, ln2_g, ln2_b):
    cos, sin = rope_tables(positions)
    for l in range(DEPTH_2):
        x = hybrid_layer(x, cos, sin, w_in[l], w_pool[l], pool_scale[l], attn_sinks[l],
                         conv_w[l], w_branch_a[l], w_branch_b[l], w_branch_c[l], w_o[l],
                         ln1_g[l], ln1_b[l], w_up[l], ffn_conv_w[l], w_down[l],
                         ln2_g[l], ln2_b[l])
    return x


def setup_inputs(seed=0):
    out = dict(first_inputs(seed))
    for name, value in second_inputs(seed + 1).items():
        if name != "x":
            out[name + "_2"] = value
    return out


def reference(
    x, norm_mix_g, w_in, b_gate, rg_conv_w, rg_conv_b, rg_w_a, rg_b_a, rg_w_x, rg_b_x,
    rg_lambda, diff_lq1, diff_lk1, diff_lq2, diff_lk2, diff_subln_g, w_branch_a, w_branch_b,
    w_branch_c, w_out, norm_ffn_g, ffn_up, ffn_conv_w, ffn_conv_b, ffn_down, final_norm_g,
    positions_2, w_in_2, w_pool_2, pool_scale_2, attn_sinks_2, conv_w_2, w_branch_a_2,
    w_branch_b_2, w_branch_c_2, w_o_2, ln1_g_2, ln1_b_2, w_up_2, ffn_conv_w_2, w_down_2,
    ln2_g_2, ln2_b_2,
):
    x = first_block(
        x, norm_mix_g, w_in, b_gate, rg_conv_w, rg_conv_b, rg_w_a, rg_b_a, rg_w_x, rg_b_x,
        rg_lambda, diff_lq1, diff_lk1, diff_lq2, diff_lk2, diff_subln_g, w_branch_a, w_branch_b,
        w_branch_c, w_out, norm_ffn_g, ffn_up, ffn_conv_w, ffn_conv_b, ffn_down, final_norm_g,
    )
    return second_block(
        x, positions_2, w_in_2, w_pool_2, pool_scale_2, attn_sinks_2, conv_w_2, w_branch_a_2,
        w_branch_b_2, w_branch_c_2, w_o_2, ln1_g_2, ln1_b_2, w_up_2, ffn_conv_w_2, w_down_2,
        ln2_g_2, ln2_b_2,
    )


_drawn_inputs = setup_inputs


def setup_inputs(seed=0):
    import zlib

    import numpy as np

    out = dict(_drawn_inputs(seed))
    spreads = {}
    factors = {'pool_scale_2': 3.643, 'attn_sinks_2': 8.0}
    for name, (base, spread) in spreads.items():
        noise = np.random.default_rng([zlib.crc32(name.encode()), seed]).standard_normal(out[name].shape)
        drawn = base * np.exp(spread * noise) if base else spread * noise
        out[name] = jnp.asarray(drawn.astype(out[name].dtype))
    for name, factor in factors.items():
        out[name] = (out[name] * factor).astype(out[name].dtype)
    return out
```

```python
import math
from contextlib import ExitStack

import numpy as np

import concourse.bass as bass
from concourse import mybir

P = 128
S = 256
DM = 1024
KT = DM // P
HD = 64
FF = 2816
FT = FF // P
UPT = 2 * FT
NQT = S // P
LAYERS2 = 2
MOBA_H, DIFF_H = 8, 4
ALPHA = (2 * LAYERS2) ** 0.25
RMS_EPS, LN_EPS = 1e-6, 1e-5
LAM_INIT = 0.8 - 0.6 * math.exp(-0.3 * 0)
MASKED = -1e30
RING = 3

WIN1, MERGE1 = 64, 16
WIN2, MERGE2 = 38, 8
DOWN_PARTS = (8, 7, 7)
DOWN = KT * len(DOWN_PARTS)


def unit_table():
    units, start = [], {}

    def phase(name, array, tiles, parts):
        start[name] = len(units)
        for t in range(tiles):
            at = 0
            for n in parts:
                units.append((array, t, at, n))
                at += n

    phase("win1", "w_win1", WIN1, (8,))
    phase("merge1", "w_merge1", KT, (8, 8))
    phase("wout1", "w_out1", KT, (8,))
    phase("up1", "w_up1", UPT, (8,))
    phase("down1", "w_down1", KT, DOWN_PARTS)
    for l in range(LAYERS2):
        phase(f"win2{l}", f"w_win2{l}", WIN2, (8,))
        phase(f"merge2{l}", f"w_merge2{l}", KT, (8,))
        phase(f"wout2{l}", f"w_out2{l}", KT, (8,))
        phase(f"up2{l}", f"w_up2{l}", UPT, (8,))
        phase(f"down2{l}", f"w_down2{l}", KT, DOWN_PARTS)
    return units, start


UNITS, START = unit_table()
FFNS = ("1", "20", "21")

COLS = {}


def _columns():
    at = 0
    for name, n in [("norm_mix_g", KT), ("b_gate", 3 * KT), ("rg_conv", 5 * KT), ("rg_b_a", KT), ("rg_b_x", KT),
                    ("rg_lambda", KT), ("subln_g", 1), ("norm_ffn_g", KT), ("ffn_1", 4 * UPT), ("final_g", KT)]:
        COLS[name] = at
        at += n
    for l in range(LAYERS2):
        for name, n in [("pool_scale", 2), ("conv", 6), ("ln1_g", KT), ("ln1_b", KT), ("ffn_2", 3 * UPT),
                        ("ln2_g", KT), ("ln2_b", KT), ("sinks", 8)]:
            COLS[f"{name}{l}"] = at
            at += n
    COLS["lq1"], COLS["lk1"], COLS["lq2"], COLS["lk2"] = (at + HD * i for i in range(4))
    return at + 4 * HD


NCOLS = _columns()

CONST = {"ident": 0, "swap": P, "alibi": 2 * P, "slide": 5 * P, "count": 8 * P, "freq": 8 * P + 2 * S}
NCONST = CONST["freq"] + 1


def constants():
    c = np.zeros((P, NCONST), np.float32)
    c[:, 0:P] = np.eye(P)
    q, k = np.arange(P)[:, None], np.arange(P)[None, :]
    diag = np.where(k <= q, (k - q) * 8.0, MASKED)
    c[:, CONST["alibi"]:CONST["alibi"] + 3 * P] = np.concatenate([diag, (k - q - P) * 8.0, diag], 1)
    own = np.where(k <= q, 0.0, MASKED)
    c[:, CONST["slide"]:CONST["slide"] + 3 * P] = np.concatenate([own, np.where(k > q, 0.0, MASKED), own], 1)
    t = np.arange(S)
    for g, w in enumerate((2, 4, 8, 16)):
        col = CONST["count"] + (g // 2) * S
        c[(g % 2) * 64:(g % 2) * 64 + 64, col:col + S] = 1.0 / np.minimum(t + 1, w)
    half = 8
    for head in (0, 64):
        for i in range(half):
            c[head + half + i, CONST["swap"] + head + i] = -1.0
            c[head + i, CONST["swap"] + head + half + i] = 1.0
            f = np.float32(500000.0) ** (-np.float32(2 * i) / np.float32(16))
            for j in (i, half + i):
                c[head + j, CONST["freq"]] = f
    return c


def schedule():
    slots = {}

    def at(n, *step):
        slots.setdefault(n, []).append(step)

    b = START["win1"]
    for half in range(NQT):
        at(b + 12 + half, "turn_v", 0, half)
    for j in range(MOBA_H):
        at(b + 13 + j, "scores", j)
        at(b + 15 + j, "weights", j)
        at(b + 16 + j, "values", j)
    for half in range(NQT):
        at(b + 25 + half, "turn_v", 1, half)
    for j in range(2 * DIFF_H):
        at(b + 26 + j, "scores", MOBA_H + j)
        if j % 2:
            at(b + 28 + j, "weights", MOBA_H + j // 2)
            at(b + 29 + j, "values", MOBA_H + j // 2)
    for t in range(KT):
        at(b + 40 + t, "rg_gates", t)
    at(b + 38, "diff_stats",)
    at(b + 39, "diff_norm",)
    for t in range(KT):
        at(b + 41 + t, "rg_recip", t)
    at(b + 48, "rg_gelu",)
    at(b + 49, "rg_roots",)
    for t in range(KT):
        at(b + 50 + t, "rg_input", t)
        at(b + 51 + t, "rg_scan", t)
        at(b + 52 + t, "rg_split", t)
    for l in range(LAYERS2):
        b = START[f"win2{l}"]
        at(b + 2, "rope", l, 0)
        at(b + 3, "turn_v2", l)
        for i in range(4):
            at(b + 4 + i, "rope", l, 1 + i)
        for j in range(8):
            g = 16 + 8 * l + j
            at(b + 9 + 2 * j, "scores", g)
            at(b + 11 + 2 * j, "weights", MOBA_H + DIFF_H + 8 * l + j)
            at(b + 12 + 2 * j, "values", MOBA_H + DIFF_H + 8 * l + j)
        at(b + 14, "pool_sums", l)
        at(b + 24, "pool_mix", l)
        for t in range(2):
            at(b + 26 + t, "gated_conv", l, t)
    b = START["win1"]
    for i, name in enumerate(("prepare_scalars", "prepare_turns", "prepare_angles", "prepare_sines", "prepare_series",
                              "prepare_sum", "prepare_softplus", "prepare_cosines")):
        at(b + 1 + i, name)
    order = ("rg_split", "rg_scan", "turn_v", "turn_v2", "rope", "weights", "scores", "values")
    for steps in slots.values():
        steps.sort(key=lambda s: order.index(s[0]) if s[0] in order else len(order))
    return slots


SLOTS = schedule()


def build(nc, args, out):
    f32, r32, i32 = mybir.dt.float32, mybir.dt.float32r, mybir.dt.int32
    ALU, ACT = mybir.AluOpType, mybir.ActivationFunctionType
    ctx = ExitStack()
    with ctx:
        def sb(name, shape, dt=f32, stack=ctx):
            return stack.enter_context(nc.sbuf_tensor(name, shape, dt))

        def sem(name):
            return ctx.enter_context(nc.semaphore(name))

        raw = sb("raw", [P, RING, 8 * P])
        whi = sb("whi", [P, RING, 8 * P], r32)
        wlo = sb("wlo", [P, RING, 8 * P], r32)
        xhi = sb("xhi", [P, KT, S], r32)
        xlo = sb("xlo", [P, KT, S], r32)
        yhi = sb("yhi", [P, 16, S], r32)
        ylo = sb("ylo", [P, 16, S], r32)
        x = sb("x", [P, KT, S])
        rgw = sb("rgw", [P, 2 * KT, P])
        poolw = sb("poolw", [P, 2 * LAYERS2, P])
        const = sb("const", [P, NCONST])
        ones = sb("ones", [P, P])
        ipos = sb("ipos", [P, S], i32)
        soft = sb("soft", [P, 5, KT])
        lamdot = sb("lamdot", [P, HD])
        vec = sb("vec", [P, NCOLS])
        prob = sb("prob", [P, 4, 3 * P])
        probT = sb("probT", [P, 2, 3 * P])
        table = sb("table", [P, 2, 3 * P])
        rope_cs = sb("rope_cs", [P, 2, S])
        tmp = sb("tmp", [P, 4, S])
        root = sb("root", [P, S])
        small = sb("small", [P, 96])
        with ExitStack() as one:
            u1 = sb("u1", [P, 72, S], stack=one)
        with ExitStack() as two:
            u2 = sb("u2", [P, 44, S], stack=two)
        fhi = sb("fhi", [P, FT, S], r32)
        flo = sb("flo", [P, FT, S], r32)
        dev = sb("dev", [P, KT, S])
        ugate = sb("ugate", [P, 3, S])
        uval = sb("uval", [P, 3, S])
        fprod = sb("fprod", [P, 3, S])
        pads = sb("pads", [P, 4, 2, 16 + S])
        zpad = sb("zpad", [P, 2, 2 + S])

        QA, KA, VA, QC, KC, VC, XR, RGATE, GATE1 = 0, 4, 8, 12, 16, 20, 24, 32, 40
        va = u1[:, 64:68, :].rearrange("p a s -> p (a s)").rearrange("p (h n) -> p h n", h=2)
        vc = u1[:, 68:72, :].rearrange("p a s -> p (a s)").rearrange("p (h n) -> p h n", h=2)
        K2, V2, Q2, XC, GB, GC, GATE2, VT2 = 0, 1, 2, 8, 10, 12, 14, 38

        NEGM, ROWSUM, RECIP, SINK = 0, 8, 16, 24
        LAMS, NLAM, G08, HBA, HBX, SP2 = 32, 37, 38, 40, 48, 56
        HBG = 64

        def col(name, i=0, n=1):
            a = COLS[name] + i
            return vec[:, a:a + n]

        def cst(name, n):
            return const[:, CONST[name]:CONST[name] + n]

        ident, swap = cst("ident", P), cst("swap", P)

        bank = [ctx.enter_context(nc.psum_tensor(f"bank{i}", [P, 512], f32)) for i in range(8)]
        unit_bank = bank[0:3]
        ps_score, ps_turn, ps_out, ps_stat, ps_misc = bank[3:8]

        load_x, load_vec, load_const, load_rg, load_pos = (sem(n) for n in ("load_x", "load_vec", "load_const", "load_rg", "load_pos"))
        arrived = [sem(f"arrived{i}") for i in range(RING)]
        split_hi, split_lo = sem("split_hi"), sem("split_lo")
        unit_done = sem("unit_done")
        ones_set = sem("ones_set")
        dve_chain, act_chain, pool_chain = sem("dve_chain"), sem("act_chain"), sem("pool_chain")
        scored, logits, expd, weighted, turned, turn_read, valued, out_hi, out_read = (
            sem(n) for n in ("scored", "logits", "expd", "weighted", "turned", "turn_read", "valued", "out_hi", "out_read"))
        tabled = sem("tabled")
        vt_turned, vt_read = sem("vt_turned"), sem("vt_read")
        misc_done, misc_read = sem("misc_done"), sem("misc_read")
        squared, summed, rooted, inverted = sem("squared"), sem("summed"), sem("rooted"), sem("inverted")
        normed, x_hi, x_lo = sem("normed"), sem("x_hi"), sem("x_lo")
        res_new = sem("res_new")
        centred, dev_squared, square_used, scaled = (sem(n) for n in ("centred", "dev_squared", "square_used", "scaled"))
        rg_tanh, rg_in, rg_root, rg_hidden, rg_hi, rg_lo, rg_gelu = (
            sem(n) for n in ("rg_tanh", "rg_in", "rg_root", "rg_hidden", "rg_hi", "rg_lo", "rg_gelu"))
        rg_recip, rg_driven, rg_state = sem("rg_recip"), sem("rg_driven"), sem("rg_state")
        conv_start, tap1, conv_done = sem("conv_start"), sem("tap1"), sem("conv_done")
        gelued, product, f_hi, f_lo = sem("gelued"), sem("product"), sem("f_hi"), sem("f_lo")
        branch_read, merged, m_hi, m_lo = sem("branch_read"), sem("merged"), sem("m_hi"), sem("m_lo")
        diff_sq, diff_sum, diff_root, diff_y, diff_hi, diff_lo = (
            sem(n) for n in ("diff_sq", "diff_sum", "diff_root", "diff_y", "diff_hi", "diff_lo"))
        copied = sem("copied")
        angles, sines, roped, lam_exp, prep = sem("angles"), sem("sines"), sem("roped"), sem("lam_exp"), sem("prep")
        pooled, pool_y, pool_hi, pool_lo = sem("pooled"), sem("pool_y"), sem("pool_hi"), sem("pool_lo")
        gconv, gconv_hi, gconv_lo = sem("gconv"), sem("gconv_hi"), sem("gconv_lo")
        stored = sem("stored")
        block = ctx.enter_context(nc.Block())

        def wait(eng, s, base, it=0, per=0):
            if isinstance(it, int):
                if base + it * per > 0:
                    eng.wait_ge(s, base + it * per)
            else:
                eng.wait_ge(s, it * per + base)

        def repeat(eng, name, count, per, body, peel_first=False):
            rounds = count // per
            lo, hi = (1 if peel_first else 0), rounds - 1
            n0 = START[name]
            for i in range(lo * per):
                body(n0 + i, i, 0)
            if hi > lo:
                with eng.Fori(lo, hi) as it:
                    for i in range(per):
                        body(n0 + i, i, it)
            for i in range(hi * per, count):
                body(n0 + i, i, 0)

        def head(j):
            if j < 8:
                return u1, QA + j // 2, KA + j // 2, 64 * (j % 2), 64 * (j % 2), j + 1
            if j < 16:
                h, m = (j - 8) // 2, (j - 8) % 2
                return u1, QC + h, KC + h, 64 * m, 64 * m, 2 * (h + 1)
            i = (j - 16) % 8
            return u2, Q2 + i // 2, K2, 64 * (i % 2), 64 * (i % 2), None

        def score_heads(w):
            if w < 8:
                return [w]
            if w < 12:
                return [8 + 2 * (w - 8), 9 + 2 * (w - 8)]
            return [16 + w - 12]

        def weight_job(j):
            return j if j < 8 else 8 + (j - 8) // 2 if j < 16 else 12 + j - 16

        def outs_before(w):
            return w // 2 if w < 8 else 4 + w - 8 if w < 12 else 8 + (w - 12) // 2

        def tile(ten, t, it=0, per=0):
            return ten[:, t:t + 1, :] if isinstance(it, int) else ten[:, bass.ds(it * per + t, 1), :]

        def tap(cols, width, k, i, it):
            a = COLS[cols] + width * i + k
            return vec[:, a:a + 1] if isinstance(it, int) else vec[:, bass.ds(it * (6 * width) + a, 1)]

        def as_tile(ap):
            return ap.rearrange("p (o s) -> p o s", o=1)

        MISC = {}
        for n in sorted(SLOTS):
            for step in SLOTS[n]:
                if step[0] in ("turn_v", "turn_v2", "rg_gates", "rope", "pool_mix", "diff_stats"):
                    MISC[step] = len(MISC)

        FREE, RESULT, counts = [], {}, {}

        def results(name, n, s):
            RESULT.setdefault(name, len(FREE))
            for _ in range(n):
                counts[s.name] = counts.get(s.name, 0) + 1
                FREE.append((s, counts[s.name]))

        results("win1", 24, copied)
        results("win1", KT, conv_done)
        results("win1", 4 * KT, copied)
        results("merge1", MERGE1, branch_read)
        results("wout1", KT, res_new)
        results("up1", UPT, conv_done)
        results("down1", KT, res_new)
        for l in range(LAYERS2):
            results(f"win2{l}", WIN2, copied)
            results(f"merge2{l}", MERGE2, branch_read)
            results(f"wout2{l}", KT, res_new)
            results(f"up2{l}", UPT, conv_done)
            results(f"down2{l}", KT, res_new)

        def bank_of(r):
            return unit_bank[r % 3]

        def down_bank(name, t):
            return unit_bank[(RESULT[name] + t % 2) % 3]

        def copies_before(l):
            return 7 * KT + WIN2 * l

        BRANCH_BASE = {0: 0, KT: MERGE1, 2 * KT: MERGE1 + MERGE2}

        def branch_bank(r, which, t):
            return unit_bank[r % 3][:, which * S:(which + 1) * S] if which < 2 else (ps_stat, ps_misc)[t % 2][:, S:2 * S]

        def branch_part(base, t, branch):
            if branch == 0:
                return merged_tile(base, t)
            return tmp[:, 2 * (t % 2) + branch - 1, :]

        def merged_tile(base, t):
            return u1[:, XR + t, :] if base == 0 else u2[:, 42 + t % 2, :]

        def gate_tile(l, branch, t):
            return u1[:, GATE1 + branch * KT + t, :] if l is None else u2[:, GATE2 + branch * KT + t, :]

        NORMS = ("mix", "ffn", "final", "ln10", "ln20", "ln11", "ln21")
        XIN = {n: KT * i for i, n in enumerate(NORMS)}
        XPART = XIN
        SUM = {n: i + 1 for i, n in enumerate(NORMS)}
        SQ = {"mix": 0, "ffn": KT, "final": 2 * KT}
        LNI = {"ln10": 0, "ln20": 1, "ln11": 2, "ln21": 3}
        RES = {"ffn": 0, "final": KT, "ln10": 2 * KT, "ln20": 3 * KT, "ln11": 4 * KT, "ln21": 5 * KT}

        @block.sync
        def _(sp):
            sp.dma_start(x[:], args["x"]).then_inc(load_x, 16)
            sp.dma_start(vec[:], args["vec"]).then_inc(load_vec, 16)

            def load(n, it=0, per=0):
                array, t, first, blocks = UNITS[n]
                wait(sp, split_lo, n - RING + 1, it, per)
                tiles = per // len(DOWN_PARTS) if array.startswith("w_down") else per
                src = args[array][t:t + 1] if isinstance(it, int) else args[array][bass.ds(it * tiles + t, 1)]
                sp.dma_start(raw[:, n % RING, 0:blocks * P], src[:, :, first * P:(first + blocks) * P].rearrange(
                    "o p n -> (o p) n")).then_inc(arrived[n % RING], 16)

            def loads(name, count, per):
                repeat(sp, name, count, per, lambda n, i, it: load(n, it, per))

            for n in range(RING):
                load(n)
            sp.dma_start(const[:], args["const"]).then_inc(load_const, 16)
            sp.dma_start(ipos[:], args["positions"]).then_inc(load_pos, 16)
            sp.dma_start(rgw[:], args["rg_w"]).then_inc(load_rg, 16)
            sp.dma_start(poolw[:], args["pool_w"]).then_inc(load_rg, 16)
            for n in range(RING, WIN1 + MERGE1):
                load(n)
            loads("wout1", KT, 3)
            loads("up1", UPT, 6)
            loads("down1", DOWN, 6)
            for l in range(LAYERS2):
                for n in range(START[f"win2{l}"], START[f"merge2{l}"]):
                    load(n)
                loads(f"merge2{l}", MERGE2, 3)
                loads(f"wout2{l}", KT, 3)
                loads(f"up2{l}", UPT, 6)
                loads(f"down2{l}", DOWN, 6)
            for t in range(KT):
                sp.wait_ge(normed, XIN["ln21"] + t + 1)
                sp.dma_start(out[:, t, :], x[:, t, :]).then_inc(stored, 16)
            sp.wait_ge(stored, 16 * KT)

        @block.gpsimd
        def _(pool):
            count = [0]

            def link(ins):
                count[0] += 1
                ins.then_inc(pool_chain, 1)
                pool.wait_ge(pool_chain, count[0])

            pool.memset(ones[:], 1.0).then_inc(ones_set, 1)
            pool.wait_ge(load_const, 16)

            def step_scores(j):
                slope = head(j)[5]
                if slope is None:
                    return
                wait(pool, logits, j - 1)
                pool.tensor_scalar(table[:, j % 2, :], cst("alibi", 3 * P), 2.0 ** -slope, None, ALU.mult).then_inc(tabled, 1)

            def step_pool_sums(l):
                link(pool.memset(pads[:, :, :, 0:16], 0.0))
                pool.wait_ge(copied, copies_before(l) + 8)
                for i in range(3):
                    w = 2 ** i
                    link(pool.tensor_tensor(pads[:, i + 1, :, 2 * w - 1:16 + S], pads[:, i, :, 2 * w - 1:16 + S],
                                            pads[:, i, :, w - 1:16 + S - w], ALU.add))
                s16 = u2[64:128, 41, :]
                link(pool.tensor_tensor(s16, pads[64:128, 3, 1, 16:16 + S], pads[64:128, 3, 1, 8:8 + S], ALU.add))
                for g, (src, t) in enumerate(((pads[0:64, 1, 0, 16:16 + S], 0), (pads[64:128, 2, 0, 16:16 + S], 0),
                                              (pads[0:64, 3, 1, 16:16 + S], 1), (s16, 1))):
                    lo = 64 * (g % 2)
                    rc = const[lo:lo + 64, CONST["count"] + t * S:CONST["count"] + (t + 1) * S]
                    dst = u2[lo:lo + 64, 39 + t, :]
                    link(pool.tensor_tensor(dst, src, rc, ALU.mult))
                pool.tensor_tensor(u2[:, 39:41, :], u2[:, 39:41, :], pads[:, 0, :, 16:16 + S], ALU.subtract).then_inc(pooled, 1)

            def step_rg_input(t):
                pool.wait_ge(rg_recip, t + 1)
                pool.wait_ge(rg_in, t + 1)
                pool.wait_ge(rg_root, 1)
                xr = u1[:, XR + t, :]
                link(pool.tensor_tensor(xr, xr, u1[:, KC + t, :], ALU.mult))
                link(pool.tensor_tensor(xr, xr, u1[:, VA + t, :], ALU.mult))
                pool.tensor_scalar(u1[:, QA + t, :], u1[:, KC + t, :], 2.0, -1.0, ALU.mult, ALU.add).then_inc(rg_driven, 1)

            def step_rg_scan(t):
                pool.wait_ge(rg_state, t + 1)
                pool.wait_ge(rg_gelu, 1)
                pool.tensor_tensor(u1[:, XR + t, :], u1[:, VA + t, :], u1[:, RGATE + t, :], ALU.mult).then_inc(rg_hidden, 1)

            STEPS = {"scores": step_scores, "pool_sums": step_pool_sums, "rg_input": step_rg_input, "rg_scan": step_rg_scan}

            def steps(n):
                for name, *a in SLOTS.get(n, []):
                    if name in STEPS:
                        STEPS[name](*a)

            def ffn(f, name):
                def low(t, it=0):
                    wait(pool, f_hi, FT * f + t + 1, it, 3)
                    pool.tensor_tensor(tile(flo, t, it, 3), tile(fprod, t % 3), tile(fhi, t, it, 3).bitcast(f32), ALU.subtract) \
                        .then_inc(f_lo, 1)

                def body(n, i, it):
                    if i % 2 == 0:
                        return
                    p, t = FT * f + i // 2, i // 2
                    wait(pool, conv_done, KT + 2 * p + 2, it, 6)
                    wait(pool, gelued, p + 1, it, 3)
                    wait(pool, f_lo, p - 2, it, 3)
                    pool.tensor_tensor(tile(fprod, t % 3), tile(ugate, t % 3), tile(uval, t % 3), ALU.mult).then_inc(product, 1)
                    if t or not isinstance(it, int):
                        low(t - 1, it)

                repeat(pool, name, UPT, 6, body, peel_first=True)
                low(FT - 1)

            def merge(base, units):
                for t in range(KT):
                    m = merged_tile(base, t)
                    for branch in (2, 1):
                        done = units * t + (1 if units == 2 and branch == 2 else units)
                        pool.wait_ge(branch_read, BRANCH_BASE[base] + done)
                        ins = pool.tensor_tensor(m, m, branch_part(base, t, branch), ALU.add)
                        if branch == 1:
                            ins.then_inc(merged, 1)
                        else:
                            link(ins)

            for n in range(WIN1):
                steps(n)
            merge(0, 2)
            ffn(0, "up1")
            for l in range(LAYERS2):
                for n in range(START[f"win2{l}"], START[f"merge2{l}"]):
                    steps(n)
                merge(KT * (1 + l), 1)
                ffn(1 + l, f"up2{l}")

        @block.scalar
        def _(act):
            def hi_part(n, it=0, per=0):
                if n >= len(UNITS):
                    return
                blocks = UNITS[n][3]
                wait(act, arrived[n % RING], 16 * (n // RING + 1), it, 16 * per // RING)
                wait(act, unit_done, n - RING + 1, it, per)
                act.activation(whi[:, n % RING, 0:blocks * P], raw[:, n % RING, 0:blocks * P], ACT.Copy).then_inc(split_hi, 1)

            def norm_squares(src, which, t):
                act.activation(dev[:, t, :], src, ACT.Square).then_inc(squared, 1)

            def norm_root(which, eps, second=False):
                if second:
                    act.wait_ge(square_used, KT * (LNI[which] + 1))
                else:
                    act.wait_ge(summed, SUM[which])
                act.activation(root[:], (ps_misc if second else ps_stat)[:, 0:S], ACT.Sqrt, scale=1.0 / DM, bias=eps_col(eps)).then_inc(rooted, 1)

            def load_sqrt():
                act.activation(small[:, 90:91], small[:, 92:93], ACT.Sqrt).then_inc(act_chain, 1)
                sqrt_loads[0] += 1
                act.wait_ge(act_chain, sqrt_loads[0])

            sqrt_loads = [0]

            def eps_col(eps):
                return small[:, 92:93] if eps == RMS_EPS else small[:, 93:94]

            def norm_hi(which, src):
                for t in range(KT):
                    act.wait_ge(normed, XIN[which] + t + 1)
                    act.activation(xhi[:, t, :], src[:, t, :], ACT.Copy).then_inc(x_hi, 1)

            act.wait_ge(load_x, 16)
            for t in range(KT):
                norm_squares(x[:, t, :], "mix", t)
            act.wait_ge(prep, 1)
            hi_part(0)
            norm_root("mix", RMS_EPS)
            norm_hi("mix", dev)
            hi_part(1)
            hi_part(2)

            def step_prepare_sines():
                act.wait_ge(angles, 1)
                act.activation(rope_cs[:, 1, :], tmp[:, 0, :], ACT.Sin).then_inc(sines, 1)
                act.activation(rope_cs[:, 0, :], tmp[:, 0, :], ACT.Sin, scale=0.5).then_inc(sines, 1)
                act.wait_ge(prep, 2)
                act.activation(small[:, SP2:SP2 + KT], small[:, SP2:SP2 + KT], ACT.Exp, scale=-1.0).then_inc(lam_exp, 1)
                act.activation(small[:, LAMS + 2:LAMS + 4], small[:, LAMS:LAMS + 2], ACT.Exp).then_inc(lam_exp, 1)

            def step_turn_v(which, half):
                u = MISC[("turn_v", which, half)]
                act.wait_ge(misc_done, u + 1)
                act.activation((va, vc)[which][:, half, :], ps_misc[:], ACT.Copy).then_inc(misc_read, 1)

            def step_turn_v2(l):
                u = MISC[("turn_v2", l)]
                act.wait_ge(misc_done, u + 1)
                act.activation(u2[:, VT2, :], ps_misc[:, 0:S], ACT.Copy).then_inc(misc_read, 1)

            def step_scores(j):
                act.wait_ge(logits, j + 1)
                s = j % 4
                for q, (a, b) in enumerate(((0, P), (P, 3 * P))):
                    e = act.activation(prob[:, s, a:b], prob[:, s, a:b], ACT.Exp, bias=small[:, NEGM + 2 * s + q:NEGM + 2 * s + q + 1],
                                       accum_out=small[:, ROWSUM + 2 * s + q:ROWSUM + 2 * s + q + 1])
                if j >= 16:
                    sk = (j - 16) % 8
                    e = act.activation(small[:, SINK + 2 * s:SINK + 2 * s + 2], small[:, NEGM + 2 * s:NEGM + 2 * s + 2], ACT.Exp,
                                       bias=col(f"sinks{(j - 16) // 8}", sk))
                e.then_inc(expd, 1)

            def step_weights(w):
                act.wait_ge(turned, w + 1)
                wait(act, valued, w - 1)
                act.activation(probT[:, w % 2, :], ps_turn[:, 0:3 * P], ACT.Copy).then_inc(turn_read, 1)

            def step_values(w):
                if w < 8 and w % 2 == 0 or w >= 12 and w % 2 == 0:
                    return
                act.wait_ge(valued, w + 1)
                if w < 8:
                    act.activation(yhi[:, w // 2, :], ps_out[:, 0:S], ACT.Copy).then_inc(out_hi, 1)
                elif w < 12:
                    h = w - 8
                    act.activation(u1[:, KC + h, :], ps_out[:, 0:S], ACT.Square).then_inc(diff_sq, 1)
                    act.activation(u1[:, QC + h, :], ps_out[:, 0:S], ACT.Copy).then_inc(out_read, 1)
                else:
                    act.activation(yhi[:, 2 + ((w - 12) % 8) // 2, :], ps_out[:, 0:S], ACT.Copy).then_inc(out_hi, 1)

            def step_diff_stats():
                u = MISC[("diff_stats",)]
                act.wait_ge(misc_done, u + 1)
                act.activation(u1[:, VC:VC + 2, :].rearrange("p a s -> p (a s)"), ps_misc[:], ACT.Sqrt, scale=1.0 / P,
                               bias=eps_col(RMS_EPS)).then_inc(misc_read, 1)
                act.wait_ge(diff_sum, 1)
                act.activation(u1[:, VC + 2:VC + 4, :].rearrange("p a s -> p (a s)"), ps_out[:], ACT.Sqrt, scale=1.0 / P,
                               bias=eps_col(RMS_EPS)).then_inc(diff_root, 1)

            def step_diff_norm():
                for h in range(DIFF_H):
                    act.wait_ge(diff_y, h + 1)
                    act.activation(yhi[:, 12 + h, :], u1[:, QC + h, :], ACT.Copy).then_inc(diff_hi, 1)

            def step_rg_gates(t):
                u = MISC[("rg_gates", t)]
                act.wait_ge(misc_done, u + 1)
                wait(act, rg_in, t - 1)
                act.activation(tmp[:, t % 2, :], ps_misc[:, 0:S], ACT.Tanh, scale=0.5, bias=small[:, HBA + t:HBA + t + 1]).then_inc(rg_tanh, 1)
                act.activation(tmp[:, 2 + t % 2, :], ps_misc[:, S:2 * S], ACT.Tanh, scale=0.5, bias=small[:, HBX + t:HBX + t + 1]).then_inc(misc_read, 1)
                act.wait_ge(rg_tanh, 2 * t + 1)
                act.activation(u1[:, QA + t, :], tmp[:, t % 2, :], ACT.Tanh, scale=small[:, SP2 + t:SP2 + t + 1],
                               bias=small[:, SP2 + t:SP2 + t + 1]).then_inc(rg_tanh, 1)

            def step_rg_gelu():
                act.wait_ge(copied, 4 * KT)
                act.activation(u1[:, RGATE:RGATE + KT, :], u1[:, RGATE:RGATE + KT, :], ACT.Gelu_apprx_tanh).then_inc(rg_gelu, 1)

            def step_rg_roots():
                act.wait_ge(rg_tanh, 2 * KT)
                act.wait_ge(diff_lo, DIFF_H)
                act.activation(u1[:, VA:VA + KT, :], u1[:, QA:QA + KT, :], ACT.Sqrt).then_inc(rg_root, 1)

            def step_rg_split(t):
                act.wait_ge(rg_hidden, t + 1)
                act.activation(yhi[:, 4 + t, :], u1[:, XR + t, :], ACT.Copy).then_inc(rg_hi, 1)

            def step_pool_mix(l):
                act.wait_ge(misc_done, MISC[("pool_mix", l)] + 1)
                for t in range(2):
                    act.activation(u2[:, 39 + t, :], ps_misc[:, t * S:(t + 1) * S], ACT.Copy, scale=col(f"pool_scale{l}", t)).then_inc(
                        misc_read if t else pool_y, 1)
                act.wait_ge(pool_y, l + 1)
                act.wait_ge(misc_read, MISC[("pool_mix", l)] + 1)
                act.activation(yhi[:, 0:2, :], u2[:, 39:41, :], ACT.Copy).then_inc(pool_hi, 1)

            def step_gated_conv(l, t):
                act.wait_ge(gconv, 2 * l + t + 1)
                act.activation(yhi[:, 6 + t, :], u2[:, XC + t, :], ACT.Copy).then_inc(gconv_hi, 1)

            STEPS = {"prepare_sines": step_prepare_sines, "turn_v": step_turn_v, "turn_v2": step_turn_v2, "scores": step_scores,
                     "weights": step_weights, "values": step_values, "diff_stats": step_diff_stats, "diff_norm": step_diff_norm,
                     "rg_gates": step_rg_gates, "rg_gelu": step_rg_gelu, "rg_roots": step_rg_roots,
                     "rg_split": step_rg_split, "pool_mix": step_pool_mix, "gated_conv": step_gated_conv}

            def steps(n, last):
                early = [s for s in SLOTS.get(n, []) if s[0] == "weights"]
                late = [s for s in SLOTS.get(n, []) if s[0] != "weights"]
                for name, *a in early:
                    STEPS[name](*a)
                if n < last:
                    hi_part(n + 3)
                for name, *a in late:
                    if name in STEPS:
                        STEPS[name](*a)

            for n in range(WIN1):
                act.wait_ge(unit_done, n + 1)
                ps = bank_of(n)[:, 0:S]
                if 24 <= n < 32:
                    t = n - 24
                    act.activation(u1[:, XR + t, :], ps, ACT.Identity, scale=col("rg_conv", 5 * t + 3),
                                   bias=col("rg_conv", 5 * t + 4)).then_inc(conv_start, 1)
                elif n < 40:
                    act.activation(u1[:, n if n < 24 else RGATE + n - 32, :], ps, ACT.Copy).then_inc(copied, 1)
                else:
                    act.activation(u1[:, GATE1 + n - 40, :], ps, ACT.Tanh, scale=0.5,
                                   bias=small[:, HBG + n - 40:HBG + n - 39]).then_inc(copied, 1)
                steps(n, WIN1 - 1)

            def merge(first, per_tile, base):
                for t in range(KT + 1):
                    if t < KT:
                        for u in range(per_tile):
                            hi_part(first + per_tile * t + u + 2)
                    t -= 1
                    if t < 0:
                        continue
                    act.wait_ge(merged, base + t + 1)
                    act.activation(xhi[:, t, :], merged_tile(base, t), ACT.Copy, scale=0.5).then_inc(m_hi, 1)

            merge(START["merge1"], 2, 0)

            def wout(first, which, base, square):
                for t in range(KT):
                    hi_part(first + t + 2)
                    if t == 0:
                        load_sqrt()
                    if square:
                        act.wait_ge(res_new, base + t + 1)
                        norm_squares(x[:, t, :], which, t)

            def down(name, which, base, square):
                def body(n, i, it):
                    hi_part(n + 2, it, 6)
                    if square and i % 3 == 2:
                        t = i // 3
                        wait(act, res_new, base + t + 1, it, 2)
                        act.activation(tile(dev, t, it, 2), tile(x, t, it, 2), ACT.Square).then_inc(squared, 1)
                load_sqrt()
                repeat(act, name, DOWN, 6, body)

            def layer_norm_squares(which):
                for t in range(KT):
                    act.wait_ge(centred, KT * LNI[which] + t + 1)
                    wait(act, square_used, KT * LNI[which] + t - 3)
                    act.activation(tmp[:, t % 4, :], dev[:, t, :], ACT.Square).then_inc(dev_squared, 1)

            def ffn(f, name, cols, silu):
                def high(t, it=0):
                    wait(act, product, FT * f + t + 1, it, 3)
                    act.activation(tile(fhi, t, it, 3), tile(fprod, t % 3), ACT.Copy).then_inc(f_hi, 1)

                def body(n, i, it):
                    hi_part(n + 2, it, 6)
                    p, r = FT * f + i // 2, (i // 2) % 3
                    wait(act, unit_done, n + 1, it, 6)
                    wait(act, product, p - 2, it, 3)
                    ps, dst = bank_of(RESULT[name] + i)[:, 0:S], (ugate, uval)[i % 2][:, r, :]
                    if silu:
                        act.activation(dst, ps, ACT.Copy, scale=tap(cols, 3, 2, i, it)).then_inc(conv_start, 1)
                    else:
                        act.activation(dst, ps, ACT.Identity, scale=tap(cols, 4, 2, i, it), bias=tap(cols, 4, 3, i, it)) \
                            .then_inc(conv_start, 1)
                    if i % 2:
                        wait(act, conv_done, KT + 2 * p + 1, it, 6)
                        act.activation(ugate[:, r, :], ugate[:, r, :], ACT.Silu if silu else ACT.Gelu_apprx_tanh).then_inc(gelued, 1)
                    elif i or not isinstance(it, int):
                        high(i // 2 - 1, it)

                repeat(act, name, UPT, 6, body, peel_first=True)
                high(FT - 1)

            wout(START["wout1"], "ffn", RES["ffn"], True)
            norm_root("ffn", RMS_EPS)
            norm_hi("ffn", dev)
            ffn(0, "up1", "ffn_1", False)
            down("down1", "final", RES["final"], True)
            norm_root("final", RMS_EPS)
            norm_hi("final", x)

            for l in range(LAYERS2):
                first = START[f"win2{l}"]
                hi_part(first + 2)
                for i in range(WIN2):
                    n = first + i
                    act.wait_ge(unit_done, n + 1)
                    ps = bank_of(RESULT[f"win2{l}"] + i)[:, 0:S]
                    if i < 14:
                        if i in (6, 7):
                            dst = pads[:, 0, i - 6, 16:16 + S]
                        else:
                            dst = u2[:, i, :]
                        act.activation(dst, ps, ACT.Copy).then_inc(copied, 1)
                    else:
                        act.activation(u2[:, i, :], ps, ACT.Tanh, scale=0.5).then_inc(copied, 1)
                    steps(n, first + WIN2 - 1)
                merge(START[f"merge2{l}"], 1, KT * (1 + l))
                wout(START[f"wout2{l}"], None, 0, False)
                layer_norm_squares(f"ln1{l}")
                norm_root(f"ln1{l}", LN_EPS, True)
                norm_hi(f"ln1{l}", x)
                ffn(1 + l, f"up2{l}", f"ffn_2{l}", True)
                down(f"down2{l}", None, 0, False)
                layer_norm_squares(f"ln2{l}")
                norm_root(f"ln2{l}", LN_EPS, True)
                if l < LAYERS2 - 1:
                    norm_hi(f"ln2{l}", x)

        @block.tensor
        def _(pe):
            def product_of(ps, slot, block, hi, lo, first, last):
                w = slice(block * P, (block + 1) * P)
                pe.matmul(ps, whi[:, slot, w], hi, start=first, stop=False)
                pe.matmul(ps, whi[:, slot, w], lo, start=False, stop=False)
                return pe.matmul(ps, wlo[:, slot, w], hi, start=False, stop=last)

            def begin(n, result, it=0, per=0, rper=0):
                wait(pe, split_lo, n + 1, it, per)
                if result is not None and result >= 2:
                    ahead = 0 if isinstance(it, int) else rper
                    done, count = FREE[result - 2 + ahead]
                    wait(pe, done, count - ahead, it, rper)

            def plain(n, result, ps, it=0, per=0, rper=0, ready=None):
                begin(n, result, it, per, rper)
                for k in range(KT):
                    if ready is not None:
                        pe.wait_ge(ready[0], ready[1] + k + 1)
                    mm = product_of(ps, n % RING, k, xhi[:, k, :], xlo[:, k, :], k == 0, k == KT - 1)
                mm.then_inc(unit_done, 1)

            def stat(which, square, t, it=0):
                if square:
                    wait(pe, squared, SQ[which] + t + 1, it, 2)
                else:
                    wait(pe, res_new, RES[which] + t + 1, it, 2)
                mm = pe.matmul(as_tile(ps_stat[:, 0:S]), ones[:], tile(dev if square else x, t, it, 2),
                               start=(t == 0 and isinstance(it, int)), stop=(t == KT - 1))
                if t == KT - 1:
                    mm.then_inc(summed, 1)

            def step_turn_v(which, half):
                u = MISC[("turn_v", which, half)]
                pe.wait_ge(copied, 12 * (which + 1))
                wait(pe, misc_read, u)
                for t in range(4):
                    mm = pe.transpose(ps_misc[:, t * P:(t + 1) * P], u1[:, (VA, VC)[which] + t, half * P:(half + 1) * P], ident)
                mm.then_inc(misc_done, 1)

            def step_turn_v2(l):
                u = MISC[("turn_v2", l)]
                pe.wait_ge(copied, copies_before(l) + 2)
                wait(pe, misc_read, u)
                for half in range(NQT):
                    mm = pe.transpose(ps_misc[:, half * P:(half + 1) * P], u2[:, V2, half * P:(half + 1) * P], ident)
                mm.then_inc(misc_done, 1)

            def step_rope(l, i):
                u = MISC[("rope", l, i)]
                tile = K2 if i == 0 else Q2 + i - 1
                pe.wait_ge(copied, copies_before(l) + tile + 1)
                wait(pe, misc_read, u)
                pe.matmul(ps_misc[:, 0:S], swap, u2[:, tile, :], start=True, stop=True).then_inc(misc_done, 1)

            def step_scores(j):
                u, q, k, qp, kp, slope = head(j)
                if j < 16:
                    pe.wait_ge(copied, 12 if j < 8 else 24)
                else:
                    i = (j - 16) % 8
                    pe.wait_ge(roped, 5 * ((j - 16) // 8) + 2 + i // 2)
                wait(pe, logits, j)
                pe.matmul(ps_score[:, 0:P], u[qp:qp + HD, q, 0:P], u[kp:kp + HD, k, 0:P], start=True, stop=True)
                pe.matmul(ps_score[:, P:3 * P], u[qp:qp + HD, q, P:2 * P], u[kp:kp + HD, k, :], start=True, stop=True,
                          skip_group_check=True).then_inc(scored, 1)

            def step_weights(w):
                pe.wait_ge(weighted, w + 1)
                wait(pe, turn_read, w)
                s = score_heads(w)[0] % 4
                for i in range(3):
                    mm = pe.transpose(ps_turn[:, i * P:(i + 1) * P], prob[:, s, i * P:(i + 1) * P], ident)
                mm.then_inc(turned, 1)

            def step_values(w):
                pe.wait_ge(turn_read, w + 1)
                if w < 8:
                    pe.wait_ge(misc_read, MISC[("turn_v", 0, 1)] + 1)
                    v, c, m, off = va, (w * HD), HD, HD * (w % 2)
                elif w < 12:
                    pe.wait_ge(misc_read, MISC[("turn_v", 1, 1)] + 1)
                    v, c, m, off = vc, (w - 8) * P, P, 0
                else:
                    i = (w - 12) % 8
                    pe.wait_ge(misc_read, MISC[("turn_v2", (w - 12) // 8)] + 1)
                    v = u2[:, VT2, :].rearrange("p (h n) -> p h n", h=2)
                    c, m, off = HD * (i % 2), HD, HD * (i % 2)
                wait(pe, out_read, outs_before(w))
                pe.matmul(ps_out[off:off + m, 0:S], v[:, 0, c:c + m], probT[:, w % 2, 0:S], start=True, stop=False)
                pe.matmul(ps_out[off:off + m, P:S], v[:, 1, c:c + m], probT[:, w % 2, S:3 * P], start=False, stop=True).then_inc(valued, 1)

            def step_diff_stats():
                u = MISC[("diff_stats",)]
                wait(pe, misc_read, u)
                pe.wait_ge(diff_sq, DIFF_H)
                pe.wait_ge(out_read, 8)
                for h in range(DIFF_H):
                    ps = (ps_misc, ps_out)[h // 2][:, (h % 2) * S:(h % 2) * S + S]
                    mm = pe.matmul(ps, ones[:], u1[:, KC + h, :], start=True, stop=True, skip_group_check=True)
                    if h == 1:
                        mm.then_inc(misc_done, 1)
                mm.then_inc(diff_sum, 1)

            def step_rg_gates(t):
                u = MISC[("rg_gates", t)]
                if t == 0:
                    pe.wait_ge(load_rg, 32)
                pe.wait_ge(conv_done, t + 1)
                wait(pe, misc_read, u)
                for g in range(2):
                    mm = pe.matmul(ps_misc[:, g * S:(g + 1) * S], rgw[:, g * KT + t, :], u1[:, XR + t, :], start=True, stop=True,
                                   skip_group_check=True)
                mm.then_inc(misc_done, 1)

            def step_pool_mix(l):
                u = MISC[("pool_mix", l)]
                pe.wait_ge(pooled, l + 1)
                wait(pe, misc_read, u)
                for t in range(2):
                    mm = pe.matmul(ps_misc[:, t * S:(t + 1) * S], poolw[:, 2 * l + t, :], u2[:, 39 + t, :], start=True, stop=True,
                                   skip_group_check=True)
                mm.then_inc(misc_done, 1)

            STEPS = {"turn_v": step_turn_v, "turn_v2": step_turn_v2, "rope": step_rope, "scores": step_scores,
                     "weights": step_weights, "values": step_values, "diff_stats": step_diff_stats,
                     "rg_gates": step_rg_gates, "pool_mix": step_pool_mix}

            def steps(n):
                for name, *a in SLOTS.get(n, []):
                    if name in STEPS:
                        STEPS[name](*a)

            def merge(first, result, units, ready):
                n, r = first, result
                for t in range(KT):
                    for parts in units:
                        begin(n, r)
                        if t == 0:
                            for s, v in ready:
                                pe.wait_ge(s, v)
                        b = 0
                        for which, (y, blocks) in enumerate(parts):
                            ps = branch_bank(r, which, t)
                            for k in range(blocks):
                                mm = product_of(ps, n % RING, b, yhi[:, y + k, :], ylo[:, y + k, :], k == 0, k == blocks - 1)
                                b += 1
                        mm.then_inc(unit_done, 1)
                        n, r = n + 1, r + 1

            def wout(name, base, which, square):
                for t in range(KT):
                    r = RESULT[name] + t
                    plain(START[name] + t, r, bank_of(r)[:, 0:S], ready=(m_lo, base) if t == 0 else None)
                    if t:
                        stat(which, square, t - 1)
                stat(which, square, KT - 1)

            def up(name, which):
                def body(n, i, it):
                    r = RESULT[name] + i
                    plain(n, r, bank_of(r)[:, 0:S], it, 6, 6, ready=(x_lo, XPART[which]) if i == 0 and isinstance(it, int) else None)
                repeat(pe, name, UPT, 6, body, peel_first=True)

            def down(name, f, which, square):
                def body(n, i, it):
                    t, part = i // len(DOWN_PARTS), i % len(DOWN_PARTS)
                    begin(n, RESULT[name] + t if part == 0 else None, it, 6, 2)
                    k0 = sum(DOWN_PARTS[:part])
                    if t == 0 and isinstance(it, int):
                        pe.wait_ge(f_lo, FT * f + k0 + DOWN_PARTS[part])
                    for k in range(DOWN_PARTS[part]):
                        mm = product_of(down_bank(name, t)[:, 0:S], n % RING, k, fhi[:, k0 + k, :], flo[:, k0 + k, :],
                                        k0 + k == 0, k0 + k == FT - 1)
                    mm.then_inc(unit_done, 1)
                    if part == 0 and (t or not isinstance(it, int)):
                        stat(which, square, t - 1, it)
                repeat(pe, name, DOWN, 6, body, peel_first=True)
                stat(which, square, KT - 1)

            def ln_squares(which):
                for t in range(KT):
                    pe.wait_ge(dev_squared, KT * LNI[which] + t + 1)
                    pe.matmul(ps_misc[:, 0:S], ones[:], tmp[:, t % 4, :], start=(t == 0), stop=(t == KT - 1)).then_inc(square_used, 1)

            pe.wait_ge(ones_set, 1)
            for t in range(KT):
                stat("mix", True, t)
            for n in range(WIN1):
                plain(n, n, bank_of(n)[:, 0:S], ready=(x_lo, 0) if n == 0 else None)
                if n == 12:
                    pe.wait_ge(load_const, 16)
                steps(n)
            merge(START["merge1"], RESULT["merge1"], [[(0, 4), (12, 4)], [(4, 8)]],
                  [(out_read, DIFF_H + MOBA_H // 2), (diff_lo, DIFF_H), (rg_lo, KT)])
            wout("wout1", 0, "ffn", True)
            up("up1", "ffn")
            down("down1", 0, "final", True)
            for l in range(LAYERS2):
                name = f"win2{l}"
                for i in range(WIN2):
                    r = RESULT[name] + i
                    plain(START[name] + i, r, bank_of(r)[:, 0:S], ready=(x_lo, XPART["ln20" if l else "final"]) if i == 0 else None)
                    steps(START[name] + i)
                merge(START[f"merge2{l}"], RESULT[f"merge2{l}"], [[(0, 2), (2, 4), (6, 2)]],
                      [(out_read, 8 + 4 * (l + 1)), (pool_lo, l + 1), (gconv_lo, 2 * l + 2)])
                wout(f"wout2{l}", KT * (1 + l), f"ln1{l}", False)
                ln_squares(f"ln1{l}")
                up(f"up2{l}", f"ln1{l}")
                down(f"down2{l}", 1 + l, f"ln2{l}", False)
                ln_squares(f"ln2{l}")

        @block.vector
        def _(dve):
            count = [0]

            def link(ins):
                count[0] += 1
                ins.then_inc(dve_chain, 1)
                dve.wait_ge(dve_chain, count[0])

            def lo_part(n, it=0, per=0):
                if n >= len(UNITS):
                    return
                w = slice(0, UNITS[n][3] * P)
                wait(dve, split_hi, n + 1, it, per)
                dve.tensor_tensor(wlo[:, n % RING, w], raw[:, n % RING, w], whi[:, n % RING, w].bitcast(f32), ALU.subtract) \
                    .then_inc(split_lo, 1)

            def low(dst, src, hi, done):
                dve.tensor_tensor(dst, src, hi.bitcast(f32), ALU.subtract).then_inc(done, 1)

            def rms(which, gain, dst):
                dve.wait_ge(rooted, SUM[which])
                link(dve.reciprocal(root[:], root[:]))
                for s in range(KT + 2):
                    if s < KT:
                        dve.scalar_tensor_tensor(dst[:, s, :], x[:, s, :], col(gain, s), root[:], ALU.mult, ALU.mult).then_inc(normed, 1)
                    if s >= 2:
                        t = s - 2
                        dve.wait_ge(x_hi, XPART[which] + t + 1)
                        low(xlo[:, t, :], dst[:, t, :], xhi[:, t, :], x_lo)

            def layer_norm(which, gain, shift, last):
                dve.wait_ge(summed, SUM[which])
                for t in range(KT):
                    dve.scalar_tensor_tensor(dev[:, t, :], ps_stat[:, 0:S], -1.0 / DM, x[:, t, :], ALU.mult, ALU.add).then_inc(centred, 1)
                dve.wait_ge(rooted, SUM[which])
                link(dve.reciprocal(root[:], root[:]))
                base = KT * LNI[which]
                for s in range(KT + 3):
                    if s < KT:
                        dve.tensor_tensor(dev[:, s, :], dev[:, s, :], root[:], ALU.mult).then_inc(scaled, 1)
                    if 1 <= s <= KT:
                        t = s - 1
                        dve.wait_ge(scaled, base + t + 1)
                        dve.tensor_scalar(x[:, t, :], dev[:, t, :], col(gain, t), col(shift, t), ALU.mult, ALU.add).then_inc(normed, 1)
                    if s >= 3 and not last:
                        t = s - 3
                        dve.wait_ge(x_hi, XPART[which] + t + 1)
                        low(xlo[:, t, :], x[:, t, :], xhi[:, t, :], x_lo)

            dve.memset(small[:, 92:93], RMS_EPS)
            dve.memset(small[:, 93:94], LN_EPS).then_inc(prep, 1)
            dve.wait_ge(load_vec, 16)
            lo_part(0)
            rms("mix", "norm_mix_g", dev)
            lo_part(1)
            lo_part(2)

            neg, z, z2, poly = (soft[:, i, :] for i in range(4))

            def step_prepare_scalars():
                for at, name, n in ((HBA, "rg_b_a", KT), (HBX, "rg_b_x", KT), (HBG, "b_gate", 3 * KT)):
                    dve.tensor_scalar(small[:, at:at + n], col(name, 0, n), 0.5, None, ALU.mult)
                dve.tensor_scalar(small[:, G08:G08 + 1], col("subln_g"), 1.0 - LAM_INIT, None, ALU.mult)
                for i in range(2):
                    link(dve.tensor_tensor_reduce(out=lamdot[:], in0=col(f"lq{i + 1}", 0, HD), in1=col(f"lk{i + 1}", 0, HD), scale=1.0,
                                                  scalar=0.0, op0=ALU.mult, op1=ALU.add, accum_out=small[:, LAMS + i:LAMS + i + 1]))
                link(dve.tensor_scalar(neg, col("rg_lambda", 0, KT), -1.0, None, ALU.mult))
                dve.tensor_tensor(small[:, SP2:SP2 + KT], neg, col("rg_lambda", 0, KT), ALU.max).then_inc(prep, 1)

            def step_prepare_turns():
                dve.wait_ge(load_pos, 16)
                dve.wait_ge(load_const, 16)
                link(dve.tensor_copy(tmp[:, 1, :], ipos[:]))
                link(dve.tensor_scalar(tmp[:, 0, :], tmp[:, 1, :], cst("freq", 1), None, ALU.mult))
                link(dve.tensor_scalar(tmp[:, 1, :], tmp[:, 0, :], 1.0 / (2 * math.pi), None, ALU.mult))
                link(dve.tensor_scalar(tmp[:, 1, :], tmp[:, 1, :], ROUND, None, ALU.add))
                link(dve.tensor_scalar(tmp[:, 1, :], tmp[:, 1, :], -ROUND, None, ALU.add))

            def step_prepare_angles():
                for part in TWO_PI:
                    link(dve.scalar_tensor_tensor(tmp[:, 0, :], tmp[:, 1, :], -part, tmp[:, 0, :], ALU.mult, ALU.add))
                dve.tensor_scalar(tmp[:, 0, :], tmp[:, 0, :], PI32, -PI32, ALU.min, ALU.max).then_inc(angles, 1)

            def step_prepare_series():
                dve.wait_ge(lam_exp, 2)
                y = small[:, SP2:SP2 + KT]
                link(dve.tensor_scalar(z, y, 2.0, None, ALU.add))
                link(dve.reciprocal(z, z))
                link(dve.tensor_tensor(z, z, y, ALU.mult))
                link(dve.tensor_tensor(z2, z, z, ALU.mult))
                link(dve.tensor_scalar(poly, z2, 1.0 / 15, 1.0 / 13, ALU.mult, ALU.add))
                terms(11)

            def terms(*ds):
                for d in ds:
                    link(dve.tensor_tensor(poly, poly, z2, ALU.mult))
                    link(dve.tensor_scalar(poly, poly, 1.0 / d, None, ALU.add))

            def step_prepare_sum():
                terms(9, 7, 5, 3)

            def step_prepare_softplus():
                terms(1)
                link(dve.tensor_tensor(poly, poly, z, ALU.mult))
                link(dve.tensor_scalar(neg, neg, 0.0, 2.0, ALU.max, ALU.mult))
                link(dve.scalar_tensor_tensor(small[:, SP2:SP2 + KT], poly, 4.0, neg, ALU.mult, ALU.add))
                link(dve.tensor_tensor(small[:, NLAM:NLAM + 1], small[:, LAMS + 3:LAMS + 4], small[:, LAMS + 2:LAMS + 3], ALU.subtract))
                link(dve.tensor_scalar(small[:, NLAM:NLAM + 1], small[:, NLAM:NLAM + 1], -LAM_INIT, None, ALU.add))

            def step_prepare_cosines():
                dve.wait_ge(sines, 2)
                link(dve.tensor_tensor(rope_cs[:, 0, :], rope_cs[:, 0, :], rope_cs[:, 0, :], ALU.mult))
                link(dve.tensor_scalar(rope_cs[:, 0, :], rope_cs[:, 0, :], -2.0, 1.0, ALU.mult, ALU.add))
                dve.memset(small[:, 91:92], 0.0).then_inc(prep, 1)

            def step_scores(j):
                s = j % 4
                dve.wait_ge(scored, j + 1)
                slope = head(j)[5]
                if slope is not None:
                    dve.wait_ge(tabled, j + 1)
                    tab = table[:, j % 2, :]
                else:
                    tab = cst("slide", 3 * P)
                if j >= 4:
                    dve.wait_ge(turned, weight_job(j - 4) + 1)
                neg_max = small[:, NEGM + 2 * s:NEGM + 2 * s + 2]
                for q, (a, b) in enumerate(((0, P), (P, 3 * P))):
                    r = dve.tensor_tensor_reduce(out=prob[:, s, a:b], in0=ps_score[:, a:b], in1=tab[:, a:b], scale=HD ** -0.5,
                                                 scalar=-3.0e38, op0=ALU.add, op1=ALU.max, accum_out=neg_max[:, q:q + 1])
                link(r)
                if slope is not None:
                    dve.tensor_scalar(neg_max, neg_max, -1.0, None, ALU.mult).then_inc(logits, 1)
                else:
                    dve.tensor_scalar(neg_max, neg_max, col(f"sinks{(j - 16) // 8}", (j - 16) % 8), -1.0, ALU.max, ALU.mult).then_inc(logits, 1)

            def step_weights(w):
                js = score_heads(w)
                dve.wait_ge(expd, js[-1] + 1)
                for j in js:
                    s = j % 4
                    total = small[:, ROWSUM + 2 * s:ROWSUM + 2 * s + 2]
                    if w >= 12:
                        link(dve.tensor_tensor(total, total, small[:, SINK + 2 * s:SINK + 2 * s + 2], ALU.add))
                    link(dve.reciprocal(small[:, RECIP + 2 * s:RECIP + 2 * s + 2], total))
                s = js[0] % 4
                ranges = ((0, 0, P), (1, P, 3 * P))
                if len(js) == 2:
                    s1 = js[1] % 4
                    r1 = small[:, RECIP + 2 * s1:RECIP + 2 * s1 + 2]
                    link(dve.tensor_scalar(r1, r1, small[:, NLAM:NLAM + 1], None, ALU.mult))
                for q, a, b in ranges:
                    r = dve.tensor_scalar(prob[:, s, a:b], prob[:, s, a:b], small[:, RECIP + 2 * s + q:RECIP + 2 * s + q + 1], None, ALU.mult)
                    if len(js) == 2:
                        link(r)
                        r = dve.scalar_tensor_tensor(prob[:, s, a:b], prob[:, s1, a:b], r1[:, q:q + 1], prob[:, s, a:b], ALU.mult, ALU.add)
                r.then_inc(weighted, 1)

            def step_values(w):
                if 8 <= w < 12 or w % 2 == 0:
                    return
                i = w // 2 if w < 8 else 4 + (w - 12) // 2
                y = w // 2 if w < 8 else 2 + ((w - 12) % 8) // 2
                dve.wait_ge(out_hi, i + 1)
                low(ylo[:, y, :], ps_out[:, 0:S], yhi[:, y, :], out_read)

            def step_diff_stats():
                dve.wait_ge(misc_read, MISC[("diff_stats",)] + 1)
                dve.wait_ge(diff_root, 1)
                link(dve.reciprocal(u1[:, VC:VC + 4, :], u1[:, VC:VC + 4, :]))

            def step_diff_norm():
                for h in range(DIFF_H):
                    o = u1[:, QC + h, :]
                    dve.scalar_tensor_tensor(o, o, small[:, G08:G08 + 1], u1[:, VC + h, :], ALU.mult, ALU.mult).then_inc(diff_y, 1)
                for h in range(DIFF_H):
                    dve.wait_ge(diff_hi, h + 1)
                    low(ylo[:, 12 + h, :], u1[:, QC + h, :], yhi[:, 12 + h, :], diff_lo)

            def step_rg_gates(t):
                dve.wait_ge(misc_read, MISC[("rg_gates", t)] + 1)
                xr = u1[:, XR + t, :]
                dve.scalar_tensor_tensor(xr, tmp[:, 2 + t % 2, :], 1.0, xr, ALU.add, ALU.mult).then_inc(rg_in, 1)

            def step_rg_recip(t):
                dve.wait_ge(rg_tanh, 2 * t + 2)
                rec = u1[:, KC + t, :]
                link(dve.tensor_scalar(rec, u1[:, QA + t, :], 1.0, None, ALU.add))
                dve.reciprocal(rec, rec).then_inc(rg_recip, 1)

            def step_rg_scan(t):
                dve.wait_ge(rg_driven, t + 1)
                dve.tensor_tensor_scan(u1[:, VA + t, :], u1[:, QA + t, :], u1[:, XR + t, :], 0.0, ALU.mult, ALU.add).then_inc(rg_state, 1)

            def step_rg_split(t):
                dve.wait_ge(rg_hi, t + 1)
                low(ylo[:, 4 + t, :], u1[:, XR + t, :], yhi[:, 4 + t, :], rg_lo)

            def step_rope(l, i):
                dve.wait_ge(misc_done, MISC[("rope", l, i)] + 1)
                t = u2[:, K2 if i == 0 else Q2 + i - 1, :]
                wait(dve, roped, 5 * l + i)
                dve.tensor_tensor(tmp[:, 3, :], ps_misc[:, 0:S], rope_cs[:, 1, :], ALU.mult).then_inc(misc_read, 1)
                link(dve.tensor_tensor(t, t, rope_cs[:, 0, :], ALU.mult))
                dve.wait_ge(misc_read, MISC[("rope", l, i)] + 1)
                dve.tensor_tensor(t, t, tmp[:, 3, :], ALU.add).then_inc(roped, 1)

            def step_pool_mix(l):
                dve.wait_ge(pool_hi, l + 1)
                dve.tensor_tensor(ylo[:, 0:2, :], u2[:, 39:41, :], yhi[:, 0:2, :].bitcast(f32), ALU.subtract).then_inc(pool_lo, 1)

            def step_gated_conv(l, t):
                dve.wait_ge(copied, copies_before(l) + 14)
                if t == 0:
                    link(dve.memset(zpad[:, :, 0:2], 0.0))
                y, z = u2[:, XC + t, :], zpad[:, t, :]
                link(dve.tensor_tensor(z[:, 2:], u2[:, GC + t, :], y, ALU.mult))
                link(dve.tensor_scalar(y, z[:, 2:], col(f"conv{l}", 3 * t + 2), None, ALU.mult))
                for k in (1, 0):
                    link(dve.scalar_tensor_tensor(y, z[:, k:k + S], col(f"conv{l}", 3 * t + k), y, ALU.mult, ALU.add))
                dve.tensor_tensor(y, y, u2[:, GB + t, :], ALU.mult).then_inc(gconv, 1)
                dve.wait_ge(gconv_hi, 2 * l + t + 1)
                low(ylo[:, 6 + t, :], y, yhi[:, 6 + t, :], gconv_lo)

            STEPS = {"prepare_scalars": step_prepare_scalars, "prepare_turns": step_prepare_turns,
                     "prepare_angles": step_prepare_angles, "prepare_series": step_prepare_series,
                     "prepare_sum": step_prepare_sum, "prepare_softplus": step_prepare_softplus,
                     "prepare_cosines": step_prepare_cosines, "scores": step_scores, "weights": step_weights, "values": step_values,
                     "diff_stats": step_diff_stats, "diff_norm": step_diff_norm, "rg_gates": step_rg_gates, "rg_recip": step_rg_recip, "rg_scan": step_rg_scan,
                     "rg_split": step_rg_split, "rope": step_rope, "pool_mix": step_pool_mix, "gated_conv": step_gated_conv}

            def steps(n, last):
                for name, *a in SLOTS.get(n + 1, []):
                    if name == "weights":
                        STEPS[name](*a)
                if n < last:
                    lo_part(n + 3)
                for name, *a in SLOTS.get(n, []):
                    if name in STEPS and name != "weights":
                        STEPS[name](*a)

            def merge(l, first, result, units, base):
                def split(t):
                    dve.wait_ge(m_hi, base + t + 1)
                    dve.scalar_tensor_tensor(xlo[:, t, :], merged_tile(base, t), 0.5, xhi[:, t, :].bitcast(f32), ALU.mult,
                                             ALU.subtract).then_inc(m_lo, 1)

                n, r = first, result
                for t in range(KT):
                    for unit, branches in enumerate(units):
                        lo_part(n + 2)
                        if unit == len(units) - 1 and t:
                            split(t - 1)
                        dve.wait_ge(unit_done, n + 1)
                        if t >= 2:
                            dve.wait_ge(merged, base + t - 1)
                        for which, branch in enumerate(branches):
                            ins = dve.scalar_tensor_tensor(branch_part(base, t, branch), gate_tile(l, branch, t), 1.0,
                                                           branch_bank(r, which, t), ALU.add, ALU.mult)
                        ins.then_inc(branch_read, 1)
                        n, r = n + 1, r + 1
                split(KT - 1)

            def residual(name, t, n, alpha, bank, it=0, per=0, tiles=0):
                wait(dve, unit_done, n + 1, it, per)
                dve.scalar_tensor_tensor(tile(x, t, it, tiles), tile(x, t, it, tiles), alpha, as_tile(bank[:, 0:S]), ALU.mult, ALU.add) \
                    .then_inc(res_new, 1)

            def wout(name, alpha):
                for t in range(KT):
                    lo_part(START[name] + t + 2)
                    residual(name, t, START[name] + t, alpha, bank_of(RESULT[name] + t))

            def up(f, name, cols, width):
                def body(n, i, it):
                    lo_part(n + 2, it, 6)
                    q = KT + UPT * f + i
                    dst = (ugate, uval)[i % 2][:, (i // 2) % 3, :]
                    ps = bank_of(RESULT[name] + i)
                    wait(dve, conv_start, q + 1, it, 6)
                    dve.scalar_tensor_tensor(dst[:, 1:], ps[:, 0:S - 1], tap(cols, width, 1, i, it), dst[:, 1:], ALU.mult, ALU.add) \
                        .then_inc(tap1, 1)
                    wait(dve, tap1, q - KT + 1, it, 6)
                    dve.scalar_tensor_tensor(dst[:, 2:], ps[:, 0:S - 2], tap(cols, width, 0, i, it), dst[:, 2:], ALU.mult, ALU.add) \
                        .then_inc(conv_done, 1)
                repeat(dve, name, UPT, 6, body, peel_first=True)

            def down(name, alpha):
                def body(n, i, it):
                    lo_part(n + 2, it, 6)
                    if i % 3 == 2:
                        residual(name, i // 3, n, alpha, down_bank(name, i // 3), it, 6, 2)
                repeat(dve, name, DOWN, 6, body)

            for n in range(WIN1):
                if 24 <= n < 32:
                    t = n - 24
                    ps, xr = bank_of(n), u1[:, XR + t, :]
                    dve.wait_ge(conv_start, t + 1)
                    for back in (1, 2):
                        link(dve.scalar_tensor_tensor(xr[:, back:], ps[:, 0:S - back], col("rg_conv", 5 * t + 3 - back), xr[:, back:],
                                                      ALU.mult, ALU.add))
                    dve.scalar_tensor_tensor(xr[:, 3:], ps[:, 0:S - 3], col("rg_conv", 5 * t), xr[:, 3:], ALU.mult, ALU.add) \
                        .then_inc(conv_done, 1)
                steps(n, WIN1 - 1)
            merge(None, START["merge1"], RESULT["merge1"], [(0, 2), (1,)], 0)
            wout("wout1", 1.0)
            rms("ffn", "norm_ffn_g", dev)
            up(0, "up1", "ffn_1", 4)
            down("down1", 1.0)
            rms("final", "final_g", x)
            for l in range(LAYERS2):
                lo_part(START[f"win2{l}"] + 2)
                for n in range(START[f"win2{l}"], START[f"merge2{l}"]):
                    steps(n, START[f"merge2{l}"] - 1)
                merge(l, START[f"merge2{l}"], RESULT[f"merge2{l}"], [(0, 1, 2)], KT * (1 + l))
                wout(f"wout2{l}", ALPHA)
                layer_norm(f"ln1{l}", f"ln1_g{l}", f"ln1_b{l}", False)
                up(1 + l, f"up2{l}", f"ffn_2{l}", 3)
                down(f"down2{l}", ALPHA)
                layer_norm(f"ln2{l}", f"ln2_g{l}", f"ln2_b{l}", l == LAYERS2 - 1)


ROUND = 1.5 * 2.0 ** 23


def _two_pi_parts():
    parts, rest = [], 2 * math.pi
    for _ in range(4):
        e = math.floor(math.log2(rest)) - 9
        p = math.floor(rest / 2.0 ** e) * 2.0 ** e
        parts.append(p)
        rest -= p
    return parts


TWO_PI = _two_pi_parts()
PI32 = 3.1415925


def _tiles(w):
    k, n = w.shape
    return np.ascontiguousarray(w.reshape(k // P, P, n // P, P).transpose(2, 1, 0, 3).reshape(n // P, P, k))


def _cols(v):
    return v.reshape(-1, P).T


def _block_diagonal(w):
    t = w.shape[0] // 2
    out = np.zeros((P, t, P), w.dtype)
    for i in range(2 * t):
        h = 64 * (i % 2)
        out[h:h + 64, i // 2, h:h + 64] = w[i]
    return out


def _interleave(a):
    s = a.shape[:-1]
    return a.reshape(*s, 2, FT, P).swapaxes(-3, -2).reshape(*s, 2 * FF)


def _heads_in_pairs(a):
    s = a.shape[:-1]
    return a.reshape(*s, 2, 4, HD).swapaxes(-3, -2).reshape(*s, 8 * HD)


def layout(g):
    out = {"x": np.ascontiguousarray(g["x"][0].T.reshape(KT, P, S).transpose(1, 0, 2)), "const": constants()}
    w = {"w_win1": _tiles(g["w_in"][0])}
    a, b, c = (_tiles(g[f"w_branch_{n}"][0]) for n in "abc")
    w["w_merge1"] = np.concatenate([a, c, b], 2)
    w["w_out1"] = _tiles(g["w_out"][0])
    w["w_up1"] = _tiles(_interleave(g["ffn_up"][0]))
    w["w_down1"] = _tiles(g["ffn_down"][0])
    vec = np.zeros((P, NCOLS), np.float32)

    def put(name, cols):
        vec[:, COLS[name]:COLS[name] + cols.shape[1]] = cols

    def by_tile(rows):
        return np.stack([_cols(r) for r in rows], 2).reshape(P, -1)

    put("norm_mix_g", _cols(g["norm_mix_g"][0]))
    put("b_gate", _cols(g["b_gate"][0]))
    put("rg_conv", by_tile([*g["rg_conv_w"][0], g["rg_conv_b"][0]]))
    for name in ("rg_b_a", "rg_b_x", "rg_lambda", "norm_ffn_g"):
        put(name, _cols(g[name][0]))
    put("subln_g", _cols(g["diff_subln_g"][0]))
    put("final_g", _cols(g["final_norm_g"]))
    put("ffn_1", by_tile([_interleave(r) for r in (*g["ffn_conv_w"][0], g["ffn_conv_b"][0])]))
    for i in (1, 2):
        for n in "qk":
            put(f"l{n}{i}", np.broadcast_to(g[f"diff_l{n}{i}"][0], (P, HD)))
    out["rg_w"] = np.concatenate([_block_diagonal(g["rg_w_a"][0]), _block_diagonal(g["rg_w_x"][0])], 1)
    pool = []
    for l in range(LAYERS2):
        w_in = g["w_in_2"][l]
        u, q, k, v, xc, gb, gc, gates = np.split(w_in, np.cumsum([256, 512, 128, 128, 256, 256, 256]), 1)
        w[f"w_win2{l}"] = _tiles(np.concatenate([k, v, _heads_in_pairs(q), u, xc, gb, gc, gates], 1))
        a, b, c = g["w_branch_a_2"][l], g["w_branch_b_2"][l], g["w_branch_c_2"][l]
        w[f"w_merge2{l}"] = np.concatenate([_tiles(a), _tiles(_heads_in_pairs(b.T).T), _tiles(c)], 2)
        w[f"w_out2{l}"] = _tiles(g["w_o_2"][l])
        w[f"w_up2{l}"] = _tiles(_interleave(g["w_up_2"][l]))
        w[f"w_down2{l}"] = _tiles(g["w_down_2"][l])
        put(f"pool_scale{l}", _cols(g["pool_scale_2"][l]))
        put(f"conv{l}", by_tile(list(g["conv_w_2"][l])))
        put(f"ffn_2{l}", by_tile([_interleave(r) for r in g["ffn_conv_w_2"][l]]))
        for name in ("ln1_g", "ln1_b", "ln2_g", "ln2_b"):
            put(f"{name}{l}", _cols(g[f"{name}_2"][l]))
        put(f"sinks{l}", np.broadcast_to(g["attn_sinks_2"][l].reshape(2, 4).T.reshape(8), (P, 8)))
        pool.append(_block_diagonal(g["w_pool_2"][l]))
    out["pool_w"] = np.concatenate(pool, 1)
    out["positions"] = np.ascontiguousarray(np.broadcast_to(g["positions_2"], (P, S)))
    return {**out, "vec": vec, **w}


def kernel(**inputs):
    import concourse.bacc as bacc
    from concourse.bass_utils import run_bass_kernel_spmd

    arrays = layout({k: np.asarray(v) for k, v in inputs.items()})
    nc = bacc.Bacc("TRN2", target_bir_lowering=False, num_devices=1)
    args = {n: nc.dram_tensor(f"in_{n}", a.shape, mybir.dt.from_np(a.dtype), kind="ExternalInput").ap() for n, a in arrays.items()}
    out = nc.dram_tensor("out_x", (P, KT, S), mybir.dt.float32, kind="ExternalOutput").ap()
    build(nc, args, out)
    r = run_bass_kernel_spmd(nc, [{f"in_{n}": a for n, a in arrays.items()}], core_ids=[0])
    return np.ascontiguousarray(r.results[0]["out_x"].transpose(2, 1, 0).reshape(1, S, DM))
```

```python
import math
from contextlib import ExitStack

import numpy as np

import concourse.bass as bass
from concourse import mybir

P = 128
S = 256
DM = 1024
KT = DM // P
HD = 64
FF = 2816
FT = FF // P
UPT = 2 * FT
NQT = S // P
LAYERS2 = 2
MOBA_H, DIFF_H = 8, 4
ALPHA = (2 * LAYERS2) ** 0.25
RMS_EPS, LN_EPS = 1e-6, 1e-5
LAM_INIT = 0.8 - 0.6 * math.exp(-0.3 * 0)
MASKED = -1e30
RING = 3

WIN1, MERGE1 = 64, 16
WIN2, MERGE2 = 38, 8
DOWN_PARTS = (8, 7, 7)
DOWN = KT * len(DOWN_PARTS)


def unit_table():
    units, start = [], {}

    def phase(name, array, tiles, parts):
        start[name] = len(units)
        for t in range(tiles):
            at = 0
            for n in parts:
                units.append((array, t, at, n))
                at += n

    phase("win1", "w_win1", WIN1, (8,))
    phase("merge1", "w_merge1", KT, (8, 8))
    phase("wout1", "w_out1", KT, (8,))
    phase("up1", "w_up1", UPT, (8,))
    phase("down1", "w_down1", KT, DOWN_PARTS)
    for l in range(LAYERS2):
        phase(f"win2{l}", f"w_win2{l}", WIN2, (8,))
        phase(f"merge2{l}", f"w_merge2{l}", KT, (8,))
        phase(f"wout2{l}", f"w_out2{l}", KT, (8,))
        phase(f"up2{l}", f"w_up2{l}", UPT, (8,))
        phase(f"down2{l}", f"w_down2{l}", KT, DOWN_PARTS)
    return units, start


UNITS, START = unit_table()
FFNS = ("1", "20", "21")

COLS = {}


def _columns():
    at = 0
    for name, n in [("norm_mix_g", KT), ("b_gate", 3 * KT), ("rg_conv", 5 * KT), ("rg_b_a", KT), ("rg_b_x", KT),
                    ("rg_lambda", KT), ("subln_g", 1), ("norm_ffn_g", KT), ("ffn_1", 4 * UPT), ("final_g", KT)]:
        COLS[name] = at
        at += n
    for l in range(LAYERS2):
        for name, n in [("pool_scale", 2), ("conv", 6), ("ln1_g", KT), ("ln1_b", KT), ("ffn_2", 3 * UPT),
                        ("ln2_g", KT), ("ln2_b", KT), ("sinks", 8)]:
            COLS[f"{name}{l}"] = at
            at += n
    COLS["lq1"], COLS["lk1"], COLS["lq2"], COLS["lk2"] = (at + HD * i for i in range(4))
    return at + 4 * HD


NCOLS = _columns()

CONST = {"ident": 0, "swap": P, "alibi": 2 * P, "slide": 5 * P, "count": 8 * P, "freq": 8 * P + 2 * S}
NCONST = CONST["freq"] + 1


def constants():
    c = np.zeros((P, NCONST), np.float32)
    c[:, 0:P] = np.eye(P)
    q, k = np.arange(P)[:, None], np.arange(P)[None, :]
    diag = np.where(k <= q, (k - q) * 8.0, MASKED)
    c[:, CONST["alibi"]:CONST["alibi"] + 3 * P] = np.concatenate([diag, (k - q - P) * 8.0, diag], 1)
    own = np.where(k <= q, 0.0, MASKED)
    c[:, CONST["slide"]:CONST["slide"] + 3 * P] = np.concatenate([own, np.where(k > q, 0.0, MASKED), own], 1)
    t = np.arange(S)
    for g, w in enumerate((2, 4, 8, 16)):
        col = CONST["count"] + (g // 2) * S
        c[(g % 2) * 64:(g % 2) * 64 + 64, col:col + S] = 1.0 / np.minimum(t + 1, w)
    half = 8
    for head in (0, 64):
        for i in range(half):
            c[head + half + i, CONST["swap"] + head + i] = -1.0
            c[head + i, CONST["swap"] + head + half + i] = 1.0
            f = np.float32(500000.0) ** (-np.float32(2 * i) / np.float32(16))
            for j in (i, half + i):
                c[head + j, CONST["freq"]] = f
    return c


def schedule():
    slots = {}

    def at(n, *step):
        slots.setdefault(n, []).append(step)

    b = START["win1"]
    for half in range(NQT):
        at(b + 12 + half, "turn_v", 0, half)
    for j in range(MOBA_H):
        at(b + 13 + j, "scores", j)
        at(b + 15 + j, "weights", j)
        at(b + 16 + j, "values", j)
    for half in range(NQT):
        at(b + 25 + half, "turn_v", 1, half)
    for j in range(2 * DIFF_H):
        at(b + 26 + j, "scores", MOBA_H + j)
        if j % 2:
            at(b + 28 + j, "weights", MOBA_H + j // 2)
            at(b + 29 + j, "values", MOBA_H + j // 2)
    for t in range(KT):
        at(b + 40 + t, "rg_gates", t)
    at(b + 38, "diff_stats",)
    at(b + 39, "diff_norm",)
    for t in range(KT):
        at(b + 41 + t, "rg_recip", t)
    at(b + 48, "rg_gelu",)
    at(b + 49, "rg_roots",)
    for t in range(KT):
        at(b + 50 + t, "rg_input", t)
        at(b + 51 + t, "rg_scan", t)
        at(b + 52 + t, "rg_split", t)
    for l in range(LAYERS2):
        b = START[f"win2{l}"]
        at(b + 2, "rope", l, 0)
        at(b + 3, "turn_v2", l)
        for i in range(4):
            at(b + 4 + i, "rope", l, 1 + i)
        for j in range(8):
            g = 16 + 8 * l + j
            at(b + 9 + 2 * j, "scores", g)
            at(b + 11 + 2 * j, "weights", MOBA_H + DIFF_H + 8 * l + j)
            at(b + 12 + 2 * j, "values", MOBA_H + DIFF_H + 8 * l + j)
        at(b + 14, "pool_sums", l)
        at(b + 24, "pool_mix", l)
        for t in range(2):
            at(b + 26 + t, "gated_conv", l, t)
    b = START["win1"]
    for i, name in enumerate(("prepare_scalars", "prepare_turns", "prepare_angles", "prepare_sines", "prepare_series",
                              "prepare_sum", "prepare_softplus", "prepare_cosines")):
        at(b + 1 + i, name)
    order = ("rg_split", "rg_scan", "turn_v", "turn_v2", "rope", "weights", "scores", "values")
    for steps in slots.values():
        steps.sort(key=lambda s: order.index(s[0]) if s[0] in order else len(order))
    return slots


SLOTS = schedule()


def build(nc, args, out):
    f32, r32, i32 = mybir.dt.float32, mybir.dt.float32r, mybir.dt.int32
    ALU, ACT = mybir.AluOpType, mybir.ActivationFunctionType
    ctx = ExitStack()
    with ctx:
        def sb(name, shape, dt=f32, stack=ctx):
            return stack.enter_context(nc.sbuf_tensor(name, shape, dt))

        def sem(name):
            return ctx.enter_context(nc.semaphore(name))

        raw = sb("raw", [P, RING, 8 * P])
        whi = sb("whi", [P, RING, 8 * P], r32)
        wlo = sb("wlo", [P, RING, 8 * P], r32)
        xhi = sb("xhi", [P, KT, S], r32)
        xlo = sb("xlo", [P, KT, S], r32)
        yhi = sb("yhi", [P, 16, S], r32)
        ylo = sb("ylo", [P, 16, S], r32)
        x = sb("x", [P, KT, S])
        rgw = sb("rgw", [P, 2 * KT, P])
        poolw = sb("poolw", [P, 2 * LAYERS2, P])
        const = sb("const", [P, NCONST])
        ones = sb("ones", [P, P])
        ipos = sb("ipos", [P, S], i32)
        soft = sb("soft", [P, 5, KT])
        lamdot = sb("lamdot", [P, HD])
        vec = sb("vec", [P, NCOLS])
        prob = sb("prob", [P, 4, 3 * P])
        probT = sb("probT", [P, 2, 3 * P])
        table = sb("table", [P, 2, 3 * P])
        rope_cs = sb("rope_cs", [P, 2, S])
        tmp = sb("tmp", [P, 4, S])
        acc = sb("acc", [P, 2, S])
        stats = sb("stats", [P, 10])
        small = sb("small", [P, 96])
        with ExitStack() as one:
            u1 = sb("u1", [P, 72, S], stack=one)
        with ExitStack() as two:
            u2 = sb("u2", [P, 44, S], stack=two)
        fhi = sb("fhi", [P, FT, S], r32)
        flo = sb("flo", [P, FT, S], r32)
        dev = sb("dev", [P, KT, S])
        ugate = sb("ugate", [P, 3, S])
        uval = sb("uval", [P, 3, S])
        fprod = sb("fprod", [P, 3, S])
        mean_rows = fprod[:, 2, :]
        diag = fprod[:, 0:2, :]
        pads = sb("pads", [P, 4, 2, 16 + S])
        zpad = sb("zpad", [P, 2, 2 + S])

        QA, KA, VA, QC, KC, VC, XR, RGATE, GATE1 = 0, 4, 8, 12, 16, 20, 24, 32, 40
        va = u1[:, 64:68, :].rearrange("p a s -> p (a s)").rearrange("p (h n) -> p h n", h=2)
        vc = u1[:, 68:72, :].rearrange("p a s -> p (a s)").rearrange("p (h n) -> p h n", h=2)
        K2, V2, Q2, XC, GB, GC, GATE2, VT2 = 0, 1, 2, 8, 10, 12, 14, 38

        NEGM, ROWSUM, RECIP, SINK = 0, 8, 16, 24
        LAMS, NLAM, G08, HBA, HBX, SP2 = 32, 37, 38, 40, 48, 56
        HBG = 64
        DEVIATION, INVERSE, NMEAN, MEAN2, VAR = 0, 2, 4, 6, 8

        def statistic(c, n=2):
            return stats[:, c:c + n]


        def col(name, i=0, n=1):
            a = COLS[name] + i
            return vec[:, a:a + n]

        def cst(name, n):
            return const[:, CONST[name]:CONST[name] + n]

        ident, swap = cst("ident", P), cst("swap", P)

        bank = [ctx.enter_context(nc.psum_tensor(f"bank{i}", [P, 512], f32)) for i in range(8)]
        unit_bank = bank[0:3]
        ps_score, ps_turn, ps_out, ps_stat, ps_misc = bank[3:8]
        square_sums, dev_sums, shift_sum = ps_misc[:, 0:2], ps_score[:, 0:2], ps_stat[:, 0:S]
        spread_inverse, spread_mean = ps_out[:, 0:S], ps_turn[:, 0:S]

        load_vec, load_const, load_rg, load_pos, load_ident = (
            sem(n) for n in ("load_vec", "load_const", "load_rg", "load_pos", "load_ident"))
        load_x = [sem(f"load_x{i}") for i in range(KT // 2)]
        arrived = [sem(f"arrived{i}") for i in range(RING)]
        split_hi, split_lo = sem("split_hi"), sem("split_lo")
        unit_done = sem("unit_done")
        ones_set = sem("ones_set")
        dve_chain, act_chain, pool_chain = sem("dve_chain"), sem("act_chain"), sem("pool_chain")
        scored, logits, expd, weighted, turned, turn_read, valued, out_hi, out_read = (
            sem(n) for n in ("scored", "logits", "expd", "weighted", "turned", "turn_read", "valued", "out_hi", "out_read"))
        tabled = sem("tabled")
        vt_turned, vt_read = sem("vt_turned"), sem("vt_read")
        misc_done, misc_read = sem("misc_done"), sem("misc_read")
        squared, dve_squared, summed, rooted, inverted, spread = (
            sem(n) for n in ("squared", "dve_squared", "summed", "rooted", "inverted", "spread"))
        normed_dve, normed_act, x_hi, x_lo, x_lo_pool = (sem(n) for n in ("normed_dve", "normed_act", "x_hi", "x_lo", "x_lo_pool"))
        res_new = sem("res_new")
        shift_ready, centred, dev_squared, scaled = (sem(n) for n in ("shift_ready", "centred", "dev_squared", "scaled"))
        added_q, added_d = sem("added_q"), sem("added_d")
        dev_summed, mean_ready, mean_spread, mean_copied, var_ready, recentred, recentred_dve, mean_squared = (
            sem(n) for n in ("dev_summed", "mean_ready", "mean_spread", "mean_copied", "var_ready", "recentred", "recentred_dve", "mean_squared"))
        rg_tanh, rg_in, rg_root, rg_hidden, rg_hi, rg_lo, rg_gelu = (
            sem(n) for n in ("rg_tanh", "rg_in", "rg_root", "rg_hidden", "rg_hi", "rg_lo", "rg_gelu"))
        rg_recip, rg_driven, rg_state = sem("rg_recip"), sem("rg_driven"), sem("rg_state")
        conv_start, tap1, conv_done = sem("conv_start"), sem("tap1"), sem("conv_done")
        gelued, product, f_hi, f_lo = sem("gelued"), sem("product"), sem("f_hi"), sem("f_lo")
        branch_read, merged, m_hi, m_lo = sem("branch_read"), sem("merged"), sem("m_hi"), sem("m_lo")
        diff_sq, diff_sum, diff_root, diff_y, diff_hi, diff_lo = (
            sem(n) for n in ("diff_sq", "diff_sum", "diff_root", "diff_y", "diff_hi", "diff_lo"))
        copied = sem("copied")
        angles, sines, roped, lam_exp, prep = sem("angles"), sem("sines"), sem("roped"), sem("lam_exp"), sem("prep")
        pooled, pool_y, pool_hi, pool_lo = sem("pooled"), sem("pool_y"), sem("pool_hi"), sem("pool_lo")
        gconv, gconv_hi, gconv_lo = sem("gconv"), sem("gconv_hi"), sem("gconv_lo")
        stored = sem("stored")
        block = ctx.enter_context(nc.Block())

        def wait(eng, s, base, it=0, per=0):
            if isinstance(it, int):
                if base + it * per > 0:
                    eng.wait_ge(s, base + it * per)
            else:
                eng.wait_ge(s, it * per + base)

        def repeat(eng, name, count, per, body, peel_first=False):
            rounds = count // per
            lo, hi = (1 if peel_first else 0), rounds - 1
            n0 = START[name]
            for i in range(lo * per):
                body(n0 + i, i, 0)
            if hi > lo:
                with eng.Fori(lo, hi) as it:
                    for i in range(per):
                        body(n0 + i, i, it)
            for i in range(hi * per, count):
                body(n0 + i, i, 0)

        def head(j):
            if j < 8:
                return u1, QA + j // 2, KA + j // 2, 64 * (j % 2), 64 * (j % 2), j + 1
            if j < 16:
                h, m = (j - 8) // 2, (j - 8) % 2
                return u1, QC + h, KC + h, 64 * m, 64 * m, 2 * (h + 1)
            i = (j - 16) % 8
            return u2, Q2 + i // 2, K2, 64 * (i % 2), 64 * (i % 2), None

        def score_heads(w):
            if w < 8:
                return [w]
            if w < 12:
                return [8 + 2 * (w - 8), 9 + 2 * (w - 8)]
            return [16 + w - 12]

        def weight_job(j):
            return j if j < 8 else 8 + (j - 8) // 2 if j < 16 else 12 + j - 16

        def outs_before(w):
            return w // 2 if w < 8 else 4 + w - 8 if w < 12 else 8 + (w - 12) // 2

        def tile(ten, t, it=0, per=0):
            return ten[:, t:t + 1, :] if isinstance(it, int) else ten[:, bass.ds(it * per + t, 1), :]

        def tap(cols, width, k, i, it):
            a = COLS[cols] + width * i + k
            return vec[:, a:a + 1] if isinstance(it, int) else vec[:, bass.ds(it * (6 * width) + a, 1)]

        def as_tile(ap):
            return ap.rearrange("p (o s) -> p o s", o=1)

        MISC = {}
        for n in sorted(SLOTS):
            for step in SLOTS[n]:
                if step[0] in ("turn_v", "turn_v2", "rg_gates", "rope", "pool_mix", "diff_stats"):
                    MISC[step] = len(MISC)

        FREE, RESULT, counts = [], {}, {}

        def results(name, n, s):
            RESULT.setdefault(name, len(FREE))
            for _ in range(n):
                counts[s.name] = counts.get(s.name, 0) + 1
                FREE.append((s, counts[s.name]))

        results("win1", 24, copied)
        results("win1", KT, conv_done)
        results("win1", 4 * KT, copied)
        results("merge1", MERGE1, branch_read)
        results("wout1", KT, res_new)
        results("up1", UPT, conv_done)
        results("down1", KT, res_new)
        for l in range(LAYERS2):
            results(f"win2{l}", WIN2, copied)
            results(f"merge2{l}", MERGE2, branch_read)
            results(f"wout2{l}", KT, res_new)
            results(f"up2{l}", UPT, conv_done)
            results(f"down2{l}", KT, res_new)

        def bank_of(r):
            return unit_bank[r % 3]

        def down_bank(name, t):
            return unit_bank[(RESULT[name] + t % 2) % 3]

        def copies_before(l):
            return 7 * KT + WIN2 * l

        BRANCH_BASE = {0: 0, KT: MERGE1, 2 * KT: MERGE1 + MERGE2}

        def branch_bank(r, which, t):
            return unit_bank[r % 3][:, which * S:(which + 1) * S] if which < 2 else (ps_stat, ps_misc)[t % 2][:, S:2 * S]

        def branch_part(base, t, branch):
            if branch == 0:
                return merged_tile(base, t)
            return tmp[:, 2 * (t % 2) + branch - 1, :]

        def merged_tile(base, t):
            return u1[:, XR + t, :] if base == 0 else u2[:, 42 + t % 2, :]

        def gate_tile(l, branch, t):
            return u1[:, GATE1 + branch * KT + t, :] if l is None else u2[:, GATE2 + branch * KT + t, :]

        NORMS = ("mix", "ffn", "final", "ln10", "ln20", "ln11", "ln21")
        XHI = {n: KT * i for i, n in enumerate(NORMS)}
        SUM = {n: i + 1 for i, n in enumerate(NORMS)}
        SQ = {"mix": 0, "ffn": KT // 2, "final": KT // 2 + KT}
        ACCQ = {n: (KT - 2) * i for i, n in enumerate(NORMS)}
        LNI = {"ln10": 0, "ln20": 1, "ln11": 2, "ln21": 3}
        RES = {"ffn": 0, "final": KT, "ln10": 2 * KT, "ln20": 3 * KT, "ln11": 4 * KT, "ln21": 5 * KT}

        POOL_LOW = (4, 6)
        DVE_MOVES = 3
        NORMED, LOW, tally = {}, {}, {}

        def tell(s):
            tally[s.name] = tally.get(s.name, 0) + 1
            return s, tally[s.name]

        def dve_affine(which, t):
            return which not in LNI or (t in (2, 5) if which == NORMS[-1] else t % 2 == 1)

        for n in NORMS:
            for t in range(KT):
                NORMED[n, t] = tell(normed_dve if dve_affine(n, t) else normed_act)
                LOW[n, t] = tell(x_lo_pool if t in POOL_LOW else x_lo)

        def square_place(t, it):
            return as_tile(tmp[:, t % (4 if isinstance(it, int) else 2), :])

        @block.sync
        def _(sp):
            for i in range(KT // 2):
                sp.dma_start(x[:, 2 * i:2 * i + 2, :], args["x"][:, 2 * i:2 * i + 2, :]).then_inc(load_x[i], 16)
            sp.dma_start(ident, args["const"][:, 0:P]).then_inc(load_ident, 16)
            sp.dma_start(vec[:], args["vec"]).then_inc(load_vec, 16)

            def load(n, it=0, per=0):
                array, t, first, blocks = UNITS[n]
                wait(sp, split_lo, n - RING + 1, it, per)
                tiles = per // len(DOWN_PARTS) if array.startswith("w_down") else per
                src = args[array][t:t + 1] if isinstance(it, int) else args[array][bass.ds(it * tiles + t, 1)]
                sp.dma_start(raw[:, n % RING, 0:blocks * P], src[:, :, first * P:(first + blocks) * P].rearrange(
                    "o p n -> (o p) n")).then_inc(arrived[n % RING], 16)

            def loads(name, count, per):
                repeat(sp, name, count, per, lambda n, i, it: load(n, it, per))

            for n in range(RING):
                load(n)
            sp.dma_start(const[:, P:], args["const"][:, P:]).then_inc(load_const, 16)
            sp.dma_start(ipos[:], args["positions"]).then_inc(load_pos, 16)
            sp.dma_start(rgw[:], args["rg_w"]).then_inc(load_rg, 16)
            sp.dma_start(poolw[:], args["pool_w"]).then_inc(load_rg, 16)
            for n in range(RING, WIN1 + MERGE1):
                load(n)
            loads("wout1", KT, 3)
            loads("up1", UPT, 6)
            loads("down1", DOWN, 6)
            for l in range(LAYERS2):
                for n in range(START[f"win2{l}"], START[f"merge2{l}"]):
                    load(n)
                loads(f"merge2{l}", MERGE2, 3)
                loads(f"wout2{l}", KT, 3)
                loads(f"up2{l}", UPT, 6)
                loads(f"down2{l}", DOWN, 6)
            for t in range(KT):
                sp.wait_ge(*NORMED["ln21", t])
                sp.dma_start(out[:, t, :], x[:, t, :]).then_inc(stored, 16)
            sp.wait_ge(stored, 16 * KT)

        @block.gpsimd
        def _(pool):
            count = [0]

            def link(ins):
                count[0] += 1
                ins.then_inc(pool_chain, 1)
                pool.wait_ge(pool_chain, count[0])

            pool.memset(ones[:], 1.0).then_inc(ones_set, 1)

            def step_scores(j):
                slope = head(j)[5]
                if slope is None:
                    return
                if j == 0:
                    pool.wait_ge(load_const, 16)
                wait(pool, logits, j - 1)
                pool.tensor_scalar(table[:, j % 2, :], cst("alibi", 3 * P), 2.0 ** -slope, None, ALU.mult).then_inc(tabled, 1)

            def step_pool_sums(l):
                link(pool.memset(pads[:, :, :, 0:16], 0.0))
                pool.wait_ge(copied, copies_before(l) + 8)
                for i in range(3):
                    w = 2 ** i
                    link(pool.tensor_tensor(pads[:, i + 1, :, 2 * w - 1:16 + S], pads[:, i, :, 2 * w - 1:16 + S],
                                            pads[:, i, :, w - 1:16 + S - w], ALU.add))
                s16 = u2[64:128, 41, :]
                link(pool.tensor_tensor(s16, pads[64:128, 3, 1, 16:16 + S], pads[64:128, 3, 1, 8:8 + S], ALU.add))
                for g, (src, t) in enumerate(((pads[0:64, 1, 0, 16:16 + S], 0), (pads[64:128, 2, 0, 16:16 + S], 0),
                                              (pads[0:64, 3, 1, 16:16 + S], 1), (s16, 1))):
                    lo = 64 * (g % 2)
                    rc = const[lo:lo + 64, CONST["count"] + t * S:CONST["count"] + (t + 1) * S]
                    dst = u2[lo:lo + 64, 39 + t, :]
                    link(pool.tensor_tensor(dst, src, rc, ALU.mult))
                pool.tensor_tensor(u2[:, 39:41, :], u2[:, 39:41, :], pads[:, 0, :, 16:16 + S], ALU.subtract).then_inc(pooled, 1)

            def step_rg_input(t):
                pool.wait_ge(rg_recip, t + 1)
                pool.wait_ge(rg_in, t + 1)
                pool.wait_ge(rg_root, 1)
                xr = u1[:, XR + t, :]
                link(pool.tensor_tensor(xr, xr, u1[:, KC + t, :], ALU.mult))
                link(pool.tensor_tensor(xr, xr, u1[:, VA + t, :], ALU.mult))
                pool.tensor_scalar(u1[:, QA + t, :], u1[:, KC + t, :], 2.0, -1.0, ALU.mult, ALU.add).then_inc(rg_driven, 1)

            def step_rg_scan(t):
                pool.wait_ge(rg_state, t + 1)
                pool.wait_ge(rg_gelu, 1)
                pool.tensor_tensor(u1[:, XR + t, :], u1[:, VA + t, :], u1[:, RGATE + t, :], ALU.mult).then_inc(rg_hidden, 1)

            STEPS = {"scores": step_scores, "pool_sums": step_pool_sums, "rg_input": step_rg_input, "rg_scan": step_rg_scan}

            def steps(n):
                for name, *a in SLOTS.get(n, []):
                    if name in STEPS:
                        STEPS[name](*a)

            def ffn(f, name):
                def low(t, it=0):
                    wait(pool, f_hi, FT * f + t + 1, it, 3)
                    pool.tensor_tensor(tile(flo, t, it, 3), tile(fprod, t % 3), tile(fhi, t, it, 3).bitcast(f32), ALU.subtract) \
                        .then_inc(f_lo, 1)

                def body(n, i, it):
                    if i % 2 == 0:
                        return
                    p, t = FT * f + i // 2, i // 2
                    wait(pool, conv_done, KT + 2 * p + 2, it, 6)
                    wait(pool, gelued, p + 1, it, 3)
                    wait(pool, f_lo, p - 2, it, 3)
                    pool.tensor_tensor(tile(fprod, t % 3), tile(ugate, t % 3), tile(uval, t % 3), ALU.mult).then_inc(product, 1)
                    if t or not isinstance(it, int):
                        low(t - 1, it)

                repeat(pool, name, UPT, 6, body, peel_first=True)
                low(FT - 1)

            def merge(base, units):
                for t in range(KT):
                    m = merged_tile(base, t)
                    for branch in (2, 1):
                        done = units * t + (1 if units == 2 and branch == 2 else units)
                        pool.wait_ge(branch_read, BRANCH_BASE[base] + done)
                        ins = pool.tensor_tensor(m, m, branch_part(base, t, branch), ALU.add)
                        if branch == 1:
                            ins.then_inc(merged, 1)
                        else:
                            link(ins)

            def add_tile(t, sums, one, other, done, base):
                if t == 1:
                    pool.tensor_tensor(acc[:, sums, :], other, one, ALU.add).then_inc(done, 1)
                elif t > 1:
                    pool.wait_ge(done, base + t - 1)
                    pool.tensor_tensor(acc[:, sums, :], acc[:, sums, :], one, ALU.add).then_inc(done, 1)

            def low_parts(which, src):
                for t in POOL_LOW:
                    pool.wait_ge(*NORMED[which, t])
                    pool.wait_ge(x_hi, XHI[which] + t + 1)
                    pool.tensor_tensor(xlo[:, t, :], src[:, t, :], xhi[:, t, :].bitcast(f32), ALU.subtract).then_inc(x_lo_pool, 1)

            def add_squares(which):
                for t in range(KT - 1):
                    if which == "mix":
                        pool.wait_ge((squared, dve_squared)[t % 2], t // 2 + 1)
                    else:
                        pool.wait_ge(squared, SQ[which] + t + 1)
                    add_tile(t, 0, dev[:, t, :], dev[:, 0, :], added_q, ACCQ[which])

            def layer_norm(which):
                i = LNI[which]
                for t in range(KT - 1):
                    pool.wait_ge(centred, KT * i + t + 1)
                    add_tile(t, 1, dev[:, t, :], dev[:, 0, :], added_d, (KT - 2) * i)
                    pool.wait_ge(dev_squared, KT * i + t + 1)
                    ring = 2 if which[:3] == "ln2" and t < 4 else 4
                    add_tile(t, 0, tmp[:, t % ring, :], tmp[:, 0, :], added_q, ACCQ[which])
                pool.wait_ge(mean_copied, i + 1)
                for t in range(DVE_MOVES, KT):
                    if t == KT - 1:
                        pool.wait_ge(dev_squared, KT * (i + 1))
                    pool.tensor_tensor(dev[:, t, :], dev[:, t, :], mean_rows, ALU.add).then_inc(recentred, 1)

            add_squares("mix")
            low_parts("mix", dev)
            for n in range(WIN1):
                steps(n)
            merge(0, 2)
            add_squares("ffn")
            low_parts("ffn", dev)
            ffn(0, "up1")
            add_squares("final")
            low_parts("final", x)
            for l in range(LAYERS2):
                for n in range(START[f"win2{l}"], START[f"merge2{l}"]):
                    steps(n)
                merge(KT * (1 + l), 1)
                layer_norm(f"ln1{l}")
                low_parts(f"ln1{l}", x)
                ffn(1 + l, f"up2{l}")
                layer_norm(f"ln2{l}")
                if l < LAYERS2 - 1:
                    low_parts(f"ln2{l}", x)

        @block.scalar
        def _(act):
            def hi_part(n, it=0, per=0):
                if n >= len(UNITS):
                    return
                blocks = UNITS[n][3]
                wait(act, arrived[n % RING], 16 * (n // RING + 1), it, 16 * per // RING)
                wait(act, unit_done, n - RING + 1, it, per)
                act.activation(whi[:, n % RING, 0:blocks * P], raw[:, n % RING, 0:blocks * P], ACT.Copy).then_inc(split_hi, 1)

            def norm_root(which, eps):
                if which in LNI:
                    act.wait_ge(var_ready, LNI[which] + 1)
                    src, scale = statistic(VAR), 1.0
                else:
                    act.wait_ge(summed, SUM[which])
                    src, scale = square_sums, 1.0 / DM
                act.activation(statistic(DEVIATION), src, ACT.Sqrt, scale=scale, bias=eps_col(eps)).then_inc(rooted, 1)
                if which in LNI:
                    act.wait_ge(mean_spread, LNI[which] + 1)
                    act.activation(mean_rows, spread_mean, ACT.Copy).then_inc(mean_copied, 1)

            def load_sqrt():
                act.activation(small[:, 90:91], small[:, 92:93], ACT.Sqrt).then_inc(act_chain, 1)
                sqrt_loads[0] += 1
                act.wait_ge(act_chain, sqrt_loads[0])

            sqrt_loads = [0]

            def eps_col(eps):
                return small[:, 92:93] if eps == RMS_EPS else small[:, 93:94]

            def norm_affine(which, last):
                g, b = which[:3] + "_g" + which[3], which[:3] + "_b" + which[3]
                for t in range(KT):
                    if dve_affine(which, t):
                        if not last:
                            act.wait_ge(*NORMED[which, t])
                            act.activation(xhi[:, t, :], x[:, t, :], ACT.Copy).then_inc(x_hi, 1)
                        continue
                    act.wait_ge(scaled, KT * LNI[which] + t + 1)
                    if not last:
                        act.activation(xhi[:, t, :], dev[:, t, :], ACT.Identity, scale=col(g, t), bias=col(b, t)).then_inc(x_hi, 1)
                    act.activation(x[:, t, :], dev[:, t, :], ACT.Identity, scale=col(g, t), bias=col(b, t)).then_inc(normed_act, 1)

            def norm_hi(which, src):
                for t in range(KT):
                    act.wait_ge(*NORMED[which, t])
                    act.activation(xhi[:, t, :], src[:, t, :], ACT.Copy).then_inc(x_hi, 1)

            act.wait_ge(prep, 1)
            load_sqrt()
            for t in range(0, KT, 2):
                act.wait_ge(load_x[t // 2], 16)
                act.activation(dev[:, t, :], x[:, t, :], ACT.Square).then_inc(squared, 1)
            norm_root("mix", RMS_EPS)
            hi_part(0)
            norm_hi("mix", dev)
            hi_part(1)
            hi_part(2)

            def step_prepare_sines():
                act.wait_ge(angles, 1)
                act.activation(rope_cs[:, 1, :], tmp[:, 0, :], ACT.Sin).then_inc(sines, 1)
                act.activation(rope_cs[:, 0, :], tmp[:, 0, :], ACT.Sin, scale=0.5).then_inc(sines, 1)
                act.wait_ge(prep, 2)
                act.activation(small[:, SP2:SP2 + KT], small[:, SP2:SP2 + KT], ACT.Exp, scale=-1.0).then_inc(lam_exp, 1)
                act.activation(small[:, LAMS + 2:LAMS + 4], small[:, LAMS:LAMS + 2], ACT.Exp).then_inc(lam_exp, 1)

            def step_turn_v(which, half):
                u = MISC[("turn_v", which, half)]
                act.wait_ge(misc_done, u + 1)
                act.activation((va, vc)[which][:, half, :], ps_misc[:], ACT.Copy).then_inc(misc_read, 1)

            def step_turn_v2(l):
                u = MISC[("turn_v2", l)]
                act.wait_ge(misc_done, u + 1)
                act.activation(u2[:, VT2, :], ps_misc[:, 0:S], ACT.Copy).then_inc(misc_read, 1)

            def step_scores(j):
                act.wait_ge(logits, j + 1)
                s = j % 4
                for q, (a, b) in enumerate(((0, P), (P, 3 * P))):
                    e = act.activation(prob[:, s, a:b], prob[:, s, a:b], ACT.Exp, bias=small[:, NEGM + 2 * s + q:NEGM + 2 * s + q + 1],
                                       accum_out=small[:, ROWSUM + 2 * s + q:ROWSUM + 2 * s + q + 1])
                if j >= 16:
                    sk = (j - 16) % 8
                    e = act.activation(small[:, SINK + 2 * s:SINK + 2 * s + 2], small[:, NEGM + 2 * s:NEGM + 2 * s + 2], ACT.Exp,
                                       bias=col(f"sinks{(j - 16) // 8}", sk))
                e.then_inc(expd, 1)

            def step_weights(w):
                act.wait_ge(turned, w + 1)
                wait(act, valued, w - 1)
                act.activation(probT[:, w % 2, :], ps_turn[:, 0:3 * P], ACT.Copy).then_inc(turn_read, 1)

            def step_values(w):
                if w < 8 and w % 2 == 0 or w >= 12 and w % 2 == 0:
                    return
                act.wait_ge(valued, w + 1)
                if w < 8:
                    act.activation(yhi[:, w // 2, :], ps_out[:, 0:S], ACT.Copy).then_inc(out_hi, 1)
                elif w < 12:
                    h = w - 8
                    act.activation(u1[:, KC + h, :], ps_out[:, 0:S], ACT.Square).then_inc(diff_sq, 1)
                    act.activation(u1[:, QC + h, :], ps_out[:, 0:S], ACT.Copy).then_inc(out_read, 1)
                else:
                    act.activation(yhi[:, 2 + ((w - 12) % 8) // 2, :], ps_out[:, 0:S], ACT.Copy).then_inc(out_hi, 1)

            def step_diff_stats():
                u = MISC[("diff_stats",)]
                act.wait_ge(misc_done, u + 1)
                act.activation(u1[:, VC:VC + 2, :].rearrange("p a s -> p (a s)"), ps_misc[:], ACT.Sqrt, scale=1.0 / P,
                               bias=eps_col(RMS_EPS)).then_inc(misc_read, 1)
                act.wait_ge(diff_sum, 1)
                act.activation(u1[:, VC + 2:VC + 4, :].rearrange("p a s -> p (a s)"), ps_out[:], ACT.Sqrt, scale=1.0 / P,
                               bias=eps_col(RMS_EPS)).then_inc(diff_root, 1)

            def step_diff_norm():
                for h in range(DIFF_H):
                    act.wait_ge(diff_y, h + 1)
                    act.activation(yhi[:, 12 + h, :], u1[:, QC + h, :], ACT.Copy).then_inc(diff_hi, 1)

            def step_rg_gates(t):
                u = MISC[("rg_gates", t)]
                act.wait_ge(misc_done, u + 1)
                wait(act, rg_in, t - 1)
                act.activation(tmp[:, t % 2, :], ps_misc[:, 0:S], ACT.Tanh, scale=0.5, bias=small[:, HBA + t:HBA + t + 1]).then_inc(rg_tanh, 1)
                act.activation(tmp[:, 2 + t % 2, :], ps_misc[:, S:2 * S], ACT.Tanh, scale=0.5, bias=small[:, HBX + t:HBX + t + 1]).then_inc(misc_read, 1)
                act.wait_ge(rg_tanh, 2 * t + 1)
                act.activation(u1[:, QA + t, :], tmp[:, t % 2, :], ACT.Tanh, scale=small[:, SP2 + t:SP2 + t + 1],
                               bias=small[:, SP2 + t:SP2 + t + 1]).then_inc(rg_tanh, 1)

            def step_rg_gelu():
                act.wait_ge(copied, 4 * KT)
                act.activation(u1[:, RGATE:RGATE + KT, :], u1[:, RGATE:RGATE + KT, :], ACT.Gelu_apprx_tanh).then_inc(rg_gelu, 1)

            def step_rg_roots():
                act.wait_ge(rg_tanh, 2 * KT)
                act.wait_ge(diff_lo, DIFF_H)
                act.activation(u1[:, VA:VA + KT, :], u1[:, QA:QA + KT, :], ACT.Sqrt).then_inc(rg_root, 1)

            def step_rg_split(t):
                act.wait_ge(rg_hidden, t + 1)
                act.activation(yhi[:, 4 + t, :], u1[:, XR + t, :], ACT.Copy).then_inc(rg_hi, 1)

            def step_pool_mix(l):
                act.wait_ge(misc_done, MISC[("pool_mix", l)] + 1)
                for t in range(2):
                    act.activation(u2[:, 39 + t, :], ps_misc[:, t * S:(t + 1) * S], ACT.Copy, scale=col(f"pool_scale{l}", t)).then_inc(
                        misc_read if t else pool_y, 1)
                act.wait_ge(pool_y, l + 1)
                act.wait_ge(misc_read, MISC[("pool_mix", l)] + 1)
                act.activation(yhi[:, 0:2, :], u2[:, 39:41, :], ACT.Copy).then_inc(pool_hi, 1)

            def step_gated_conv(l, t):
                act.wait_ge(gconv, 2 * l + t + 1)
                act.activation(yhi[:, 6 + t, :], u2[:, XC + t, :], ACT.Copy).then_inc(gconv_hi, 1)

            STEPS = {"prepare_sines": step_prepare_sines, "turn_v": step_turn_v, "turn_v2": step_turn_v2, "scores": step_scores,
                     "weights": step_weights, "values": step_values, "diff_stats": step_diff_stats, "diff_norm": step_diff_norm,
                     "rg_gates": step_rg_gates, "rg_gelu": step_rg_gelu, "rg_roots": step_rg_roots,
                     "rg_split": step_rg_split, "pool_mix": step_pool_mix, "gated_conv": step_gated_conv}

            def steps(n, last):
                early = [s for s in SLOTS.get(n, []) if s[0] == "weights"]
                late = [s for s in SLOTS.get(n, []) if s[0] != "weights"]
                for name, *a in early:
                    STEPS[name](*a)
                if n < last:
                    hi_part(n + 3)
                for name, *a in late:
                    if name in STEPS:
                        STEPS[name](*a)

            for n in range(WIN1):
                act.wait_ge(unit_done, n + 1)
                ps = bank_of(n)[:, 0:S]
                if 24 <= n < 32:
                    t = n - 24
                    act.activation(u1[:, XR + t, :], ps, ACT.Identity, scale=col("rg_conv", 5 * t + 3),
                                   bias=col("rg_conv", 5 * t + 4)).then_inc(conv_start, 1)
                elif n < 40:
                    act.activation(u1[:, n if n < 24 else RGATE + n - 32, :], ps, ACT.Copy).then_inc(copied, 1)
                else:
                    act.activation(u1[:, GATE1 + n - 40, :], ps, ACT.Tanh, scale=0.5,
                                   bias=small[:, HBG + n - 40:HBG + n - 39]).then_inc(copied, 1)
                steps(n, WIN1 - 1)

            def merge(first, per_tile, base):
                for t in range(KT + 1):
                    if t < KT:
                        for u in range(per_tile):
                            hi_part(first + per_tile * t + u + 2)
                    t -= 1
                    if t < 0:
                        continue
                    act.wait_ge(merged, base + t + 1)
                    act.activation(xhi[:, t, :], merged_tile(base, t), ACT.Copy, scale=0.5).then_inc(m_hi, 1)

            merge(START["merge1"], 2, 0)

            def square(which, t, it=0):
                if which not in LNI:
                    wait(act, res_new, RES[which] + t + 1, it, 2)
                    act.activation(tile(dev, t, it, 2), tile(x, t, it, 2), ACT.Square).then_inc(squared, 1)
                    return
                wait(act, centred, KT * LNI[which] + t + 1, it, 2)
                if not isinstance(it, int):
                    wait(act, added_q, ACCQ[which] + t - 1, it, 2)
                elif t >= 4:
                    act.wait_ge(added_q, ACCQ[which] + t - 2)
                act.activation(square_place(t, it), tile(dev, t, it, 2), ACT.Square).then_inc(dev_squared, 1)

            def wout(first, which):
                for t in range(KT):
                    hi_part(first + t + 2)
                    if t == 0:
                        load_sqrt()
                    if which in LNI:
                        due = [] if t < 3 else [0, 1] if t == 3 else [t - 2] if t < KT - 1 else [KT - 3, KT - 2]
                    else:
                        due = [t - 1] if t else []
                    for u in due:
                        square(which, u)
                square(which, KT - 1)

            def down(name, which):
                def body(n, i, it):
                    hi_part(n + 2, it, 6)
                    if i % 3 == 1 and not (isinstance(it, int) and i < 6):
                        square(which, i // 3 - 2, it)
                load_sqrt()
                repeat(act, name, DOWN, 6, body, peel_first=True)
                square(which, KT - 2)
                square(which, KT - 1)

            def ffn(f, name, cols, silu):
                def high(t, it=0):
                    wait(act, product, FT * f + t + 1, it, 3)
                    act.activation(tile(fhi, t, it, 3), tile(fprod, t % 3), ACT.Copy).then_inc(f_hi, 1)

                def body(n, i, it):
                    hi_part(n + 2, it, 6)
                    p, r = FT * f + i // 2, (i // 2) % 3
                    wait(act, unit_done, n + 1, it, 6)
                    wait(act, product, p - 2, it, 3)
                    ps, dst = bank_of(RESULT[name] + i)[:, 0:S], (ugate, uval)[i % 2][:, r, :]
                    if silu:
                        act.activation(dst, ps, ACT.Copy, scale=tap(cols, 3, 2, i, it)).then_inc(conv_start, 1)
                    else:
                        act.activation(dst, ps, ACT.Identity, scale=tap(cols, 4, 2, i, it), bias=tap(cols, 4, 3, i, it)) \
                            .then_inc(conv_start, 1)
                    if i % 2:
                        wait(act, conv_done, KT + 2 * p + 1, it, 6)
                        act.activation(ugate[:, r, :], ugate[:, r, :], ACT.Silu if silu else ACT.Gelu_apprx_tanh).then_inc(gelued, 1)
                    elif i or not isinstance(it, int):
                        high(i // 2 - 1, it)

                repeat(act, name, UPT, 6, body, peel_first=True)
                high(FT - 1)

            wout(START["wout1"], "ffn")
            norm_root("ffn", RMS_EPS)
            norm_hi("ffn", dev)
            ffn(0, "up1", "ffn_1", False)
            down("down1", "final")
            norm_root("final", RMS_EPS)
            norm_hi("final", x)

            for l in range(LAYERS2):
                first = START[f"win2{l}"]
                hi_part(first + 2)
                for i in range(WIN2):
                    n = first + i
                    act.wait_ge(unit_done, n + 1)
                    ps = bank_of(RESULT[f"win2{l}"] + i)[:, 0:S]
                    if i < 14:
                        if i in (6, 7):
                            dst = pads[:, 0, i - 6, 16:16 + S]
                        else:
                            dst = u2[:, i, :]
                        act.activation(dst, ps, ACT.Copy).then_inc(copied, 1)
                    else:
                        act.activation(u2[:, i, :], ps, ACT.Tanh, scale=0.5).then_inc(copied, 1)
                    steps(n, first + WIN2 - 1)
                merge(START[f"merge2{l}"], 1, KT * (1 + l))
                wout(START[f"wout2{l}"], f"ln1{l}")
                norm_root(f"ln1{l}", LN_EPS)
                norm_affine(f"ln1{l}", False)
                ffn(1 + l, f"up2{l}", f"ffn_2{l}", True)
                down(f"down2{l}", f"ln2{l}")
                norm_root(f"ln2{l}", LN_EPS)
                norm_affine(f"ln2{l}", l == LAYERS2 - 1)

        @block.tensor
        def _(pe):
            def product_of(ps, slot, block, hi, lo, first, last):
                w = slice(block * P, (block + 1) * P)
                pe.matmul(ps, whi[:, slot, w], hi, start=first, stop=False)
                pe.matmul(ps, whi[:, slot, w], lo, start=False, stop=False)
                return pe.matmul(ps, wlo[:, slot, w], hi, start=False, stop=last)

            def begin(n, result, it=0, per=0, rper=0):
                wait(pe, split_lo, n + 1, it, per)
                if result is not None and result >= 2:
                    ahead = 0 if isinstance(it, int) else rper
                    done, count = FREE[result - 2 + ahead]
                    wait(pe, done, count - ahead, it, rper)

            def plain(n, result, ps, it=0, per=0, rper=0, ready=None):
                begin(n, result, it, per, rper)
                for k in range(KT):
                    if ready is not None:
                        pe.wait_ge(*ready[k])
                    mm = product_of(ps, n % RING, k, xhi[:, k, :], xlo[:, k, :], k == 0, k == KT - 1)
                mm.then_inc(unit_done, 1)

            def lows(which):
                return [LOW[which, t] for t in range(KT)]

            def token_sums(dst, sources):
                for h in range(2):
                    for i, (src, ready, count) in enumerate(sources):
                        if h == 0:
                            pe.wait_ge(ready, count)
                        mm = pe.matmul(dst[:, h:h + 1], src[:, h * P:(h + 1) * P], ones[:, 0:1], start=(i == 0),
                                       stop=(i == len(sources) - 1))
                return mm

            def spread_out(dst, i):
                return pe.matmul(dst, ones[:], diag[:, i, :], start=True, stop=True)

            def rms(which):
                last = (dve_squared, KT // 2) if which == "mix" else (squared, SQ[which] + KT)
                sources = [(acc[:, 0, :], added_q, ACCQ[which] + KT - 2), (dev[:, KT - 1, :], *last)]
                token_sums(square_sums, sources).then_inc(summed, 1)
                pe.wait_ge(inverted, SUM[which])
                spread_out(spread_inverse, 1).then_inc(spread, 1)

            def layer_norm_shift(which):
                pe.wait_ge(res_new, RES[which] + 1)
                pe.matmul(shift_sum, ones[:], x[:, 0, :], start=True, stop=True).then_inc(shift_ready, 1)

            def layer_norm(which):
                i = LNI[which]
                token_sums(dev_sums, [(acc[:, 1, :], added_d, (KT - 2) * (i + 1)), (dev[:, KT - 1, :], centred, KT * (i + 1))]) \
                    .then_inc(dev_summed, 1)
                token_sums(square_sums, [(acc[:, 0, :], added_q, ACCQ[which] + KT - 2), (tmp[:, 3, :], dev_squared, KT * (i + 1))]) \
                    .then_inc(summed, 1)
                pe.wait_ge(mean_ready, i + 1)
                spread_out(spread_mean, 0).then_inc(mean_spread, 1)
                pe.wait_ge(inverted, SUM[which])
                spread_out(spread_inverse, 1).then_inc(spread, 1)

            def step_turn_v(which, half):
                u = MISC[("turn_v", which, half)]
                pe.wait_ge(copied, 12 * (which + 1))
                wait(pe, misc_read, u)
                for t in range(4):
                    mm = pe.transpose(ps_misc[:, t * P:(t + 1) * P], u1[:, (VA, VC)[which] + t, half * P:(half + 1) * P], ident)
                mm.then_inc(misc_done, 1)

            def step_turn_v2(l):
                u = MISC[("turn_v2", l)]
                pe.wait_ge(copied, copies_before(l) + 2)
                wait(pe, misc_read, u)
                for half in range(NQT):
                    mm = pe.transpose(ps_misc[:, half * P:(half + 1) * P], u2[:, V2, half * P:(half + 1) * P], ident)
                mm.then_inc(misc_done, 1)

            def step_rope(l, i):
                u = MISC[("rope", l, i)]
                tile = K2 if i == 0 else Q2 + i - 1
                pe.wait_ge(copied, copies_before(l) + tile + 1)
                wait(pe, misc_read, u)
                pe.matmul(ps_misc[:, 0:S], swap, u2[:, tile, :], start=True, stop=True).then_inc(misc_done, 1)

            def step_scores(j):
                u, q, k, qp, kp, slope = head(j)
                if j < 16:
                    pe.wait_ge(copied, 12 if j < 8 else 24)
                else:
                    i = (j - 16) % 8
                    pe.wait_ge(roped, 5 * ((j - 16) // 8) + 2 + i // 2)
                wait(pe, logits, j)
                pe.matmul(ps_score[:, 0:P], u[qp:qp + HD, q, 0:P], u[kp:kp + HD, k, 0:P], start=True, stop=True)
                pe.matmul(ps_score[:, P:3 * P], u[qp:qp + HD, q, P:2 * P], u[kp:kp + HD, k, :], start=True, stop=True,
                          skip_group_check=True).then_inc(scored, 1)

            def step_weights(w):
                pe.wait_ge(weighted, w + 1)
                wait(pe, turn_read, w)
                s = score_heads(w)[0] % 4
                for i in range(3):
                    mm = pe.transpose(ps_turn[:, i * P:(i + 1) * P], prob[:, s, i * P:(i + 1) * P], ident)
                mm.then_inc(turned, 1)

            def step_values(w):
                pe.wait_ge(turn_read, w + 1)
                if w < 8:
                    pe.wait_ge(misc_read, MISC[("turn_v", 0, 1)] + 1)
                    v, c, m, off = va, (w * HD), HD, HD * (w % 2)
                elif w < 12:
                    pe.wait_ge(misc_read, MISC[("turn_v", 1, 1)] + 1)
                    v, c, m, off = vc, (w - 8) * P, P, 0
                else:
                    i = (w - 12) % 8
                    pe.wait_ge(misc_read, MISC[("turn_v2", (w - 12) // 8)] + 1)
                    v = u2[:, VT2, :].rearrange("p (h n) -> p h n", h=2)
                    c, m, off = HD * (i % 2), HD, HD * (i % 2)
                wait(pe, out_read, outs_before(w))
                pe.matmul(ps_out[off:off + m, 0:S], v[:, 0, c:c + m], probT[:, w % 2, 0:S], start=True, stop=False)
                pe.matmul(ps_out[off:off + m, P:S], v[:, 1, c:c + m], probT[:, w % 2, S:3 * P], start=False, stop=True).then_inc(valued, 1)

            def step_diff_stats():
                u = MISC[("diff_stats",)]
                wait(pe, misc_read, u)
                pe.wait_ge(diff_sq, DIFF_H)
                pe.wait_ge(out_read, 8)
                for h in range(DIFF_H):
                    ps = (ps_misc, ps_out)[h // 2][:, (h % 2) * S:(h % 2) * S + S]
                    mm = pe.matmul(ps, ones[:], u1[:, KC + h, :], start=True, stop=True, skip_group_check=True)
                    if h == 1:
                        mm.then_inc(misc_done, 1)
                mm.then_inc(diff_sum, 1)

            def step_rg_gates(t):
                u = MISC[("rg_gates", t)]
                if t == 0:
                    pe.wait_ge(load_rg, 32)
                pe.wait_ge(conv_done, t + 1)
                wait(pe, misc_read, u)
                for g in range(2):
                    mm = pe.matmul(ps_misc[:, g * S:(g + 1) * S], rgw[:, g * KT + t, :], u1[:, XR + t, :], start=True, stop=True,
                                   skip_group_check=True)
                mm.then_inc(misc_done, 1)

            def step_pool_mix(l):
                u = MISC[("pool_mix", l)]
                pe.wait_ge(pooled, l + 1)
                wait(pe, misc_read, u)
                for t in range(2):
                    mm = pe.matmul(ps_misc[:, t * S:(t + 1) * S], poolw[:, 2 * l + t, :], u2[:, 39 + t, :], start=True, stop=True,
                                   skip_group_check=True)
                mm.then_inc(misc_done, 1)

            STEPS = {"turn_v": step_turn_v, "turn_v2": step_turn_v2, "rope": step_rope, "scores": step_scores,
                     "weights": step_weights, "values": step_values, "diff_stats": step_diff_stats,
                     "rg_gates": step_rg_gates, "pool_mix": step_pool_mix}

            def steps(n):
                for name, *a in SLOTS.get(n, []):
                    if name in STEPS:
                        STEPS[name](*a)

            def merge(first, result, units, ready):
                n, r = first, result
                for t in range(KT):
                    for parts in units:
                        begin(n, r)
                        if t == 0:
                            for s, v in ready:
                                pe.wait_ge(s, v)
                        b = 0
                        for which, (y, blocks) in enumerate(parts):
                            ps = branch_bank(r, which, t)
                            for k in range(blocks):
                                mm = product_of(ps, n % RING, b, yhi[:, y + k, :], ylo[:, y + k, :], k == 0, k == blocks - 1)
                                b += 1
                        mm.then_inc(unit_done, 1)
                        n, r = n + 1, r + 1

            def wout(name, base, which):
                for t in range(KT):
                    r = RESULT[name] + t
                    plain(START[name] + t, r, bank_of(r)[:, 0:S], ready=[(m_lo, base + k + 1) for k in range(KT)] if t == 0 else None)
                    if t == 1 and which in LNI:
                        layer_norm_shift(which)

            def up(name, which):
                def body(n, i, it):
                    r = RESULT[name] + i
                    plain(n, r, bank_of(r)[:, 0:S], it, 6, 6, ready=lows(which) if i == 0 and isinstance(it, int) else None)
                repeat(pe, name, UPT, 6, body, peel_first=True)

            def down(name, f, which):
                def body(n, i, it):
                    t, part = i // len(DOWN_PARTS), i % len(DOWN_PARTS)
                    begin(n, RESULT[name] + t if part == 0 else None, it, 6, 2)
                    k0 = sum(DOWN_PARTS[:part])
                    if t == 0 and isinstance(it, int):
                        pe.wait_ge(f_lo, FT * f + k0 + DOWN_PARTS[part])
                    for k in range(DOWN_PARTS[part]):
                        mm = product_of(down_bank(name, t)[:, 0:S], n % RING, k, fhi[:, k0 + k, :], flo[:, k0 + k, :],
                                        k0 + k == 0, k0 + k == FT - 1)
                    mm.then_inc(unit_done, 1)
                    if which in LNI and i == len(DOWN_PARTS) and isinstance(it, int) and it == 0:
                        layer_norm_shift(which)
                repeat(pe, name, DOWN, 6, body, peel_first=True)

            pe.wait_ge(ones_set, 1)
            rms("mix")
            for n in range(WIN1):
                plain(n, n, bank_of(n)[:, 0:S], ready=lows("mix") if n == 0 else None)
                if n == 12:
                    pe.wait_ge(load_const, 16)
                steps(n)
            merge(START["merge1"], RESULT["merge1"], [[(0, 4), (12, 4)], [(4, 8)]],
                  [(out_read, DIFF_H + MOBA_H // 2), (diff_lo, DIFF_H), (rg_lo, KT)])
            wout("wout1", 0, "ffn")
            rms("ffn")
            up("up1", "ffn")
            down("down1", 0, "final")
            rms("final")
            for l in range(LAYERS2):
                name = f"win2{l}"
                for i in range(WIN2):
                    r = RESULT[name] + i
                    plain(START[name] + i, r, bank_of(r)[:, 0:S], ready=lows("ln20" if l else "final") if i == 0 else None)
                    steps(START[name] + i)
                merge(START[f"merge2{l}"], RESULT[f"merge2{l}"], [[(0, 2), (2, 4), (6, 2)]],
                      [(out_read, 8 + 4 * (l + 1)), (pool_lo, l + 1), (gconv_lo, 2 * l + 2)])
                wout(f"wout2{l}", KT * (1 + l), f"ln1{l}")
                layer_norm(f"ln1{l}")
                up(f"up2{l}", f"ln1{l}")
                down(f"down2{l}", 1 + l, f"ln2{l}")
                layer_norm(f"ln2{l}")

        @block.vector
        def _(dve):
            count = [0]

            def link(ins):
                count[0] += 1
                ins.then_inc(dve_chain, 1)
                dve.wait_ge(dve_chain, count[0])

            def lo_part(n, it=0, per=0):
                if n >= len(UNITS):
                    return
                w = slice(0, UNITS[n][3] * P)
                wait(dve, split_hi, n + 1, it, per)
                dve.tensor_tensor(wlo[:, n % RING, w], raw[:, n % RING, w], whi[:, n % RING, w].bitcast(f32), ALU.subtract) \
                    .then_inc(split_lo, 1)

            def low(dst, src, hi, done):
                dve.tensor_tensor(dst, src, hi.bitcast(f32), ALU.subtract).then_inc(done, 1)

            def on_diagonal(i, c, done):
                for h in range(2):
                    ins = dve.tensor_scalar(diag[:, i, h * P:(h + 1) * P], ident, statistic(c + h, 1), None, ALU.mult)
                ins.then_inc(done, 1)

            def invert(which):
                dve.wait_ge(rooted, SUM[which])
                link(dve.reciprocal(statistic(INVERSE), statistic(DEVIATION)))
                on_diagonal(1, INVERSE, inverted)
                if which in LNI:
                    dve.wait_ge(mean_copied, LNI[which] + 1)
                    for t in range(DVE_MOVES):
                        dve.tensor_tensor(dev[:, t, :], dev[:, t, :], mean_rows, ALU.add).then_inc(recentred_dve, 1)
                dve.wait_ge(spread, SUM[which])

            def low_part(which, t, src):
                if t in POOL_LOW:
                    return
                dve.wait_ge(x_hi, XHI[which] + t + 1)
                dve.wait_ge(*NORMED[which, t])
                low(xlo[:, t, :], src[:, t, :], xhi[:, t, :], x_lo)

            def rms(which, gain, dst):
                invert(which)
                for s in range(KT + 2):
                    if s < KT:
                        dve.scalar_tensor_tensor(dst[:, s, :], x[:, s, :], col(gain, s), spread_inverse, ALU.mult, ALU.mult) \
                            .then_inc(normed_dve, 1)
                    if s >= 2:
                        low_part(which, s - 2, dst)

            def deviation(which, t, it=0):
                wait(dve, shift_ready, LNI[which] + 1)
                wait(dve, res_new, RES[which] + t + 1, it, 2)
                dve.scalar_tensor_tensor(tile(dev, t, it, 2), as_tile(shift_sum), -1.0 / P, tile(x, t, it, 2), ALU.mult, ALU.add) \
                    .then_inc(centred, 1)

            def layer_norm(which, last):
                i = LNI[which]
                dve.wait_ge(dev_summed, i + 1)
                link(dve.tensor_scalar(statistic(NMEAN), dev_sums, -1.0 / DM, None, ALU.mult))
                on_diagonal(0, NMEAN, mean_ready)
                dve.tensor_tensor(statistic(MEAN2), statistic(NMEAN), statistic(NMEAN), ALU.mult).then_inc(mean_squared, 1)
                dve.wait_ge(mean_squared, i + 1)
                dve.wait_ge(summed, SUM[which])
                dve.scalar_tensor_tensor(statistic(VAR), square_sums, 1.0 / DM, statistic(MEAN2), ALU.mult, ALU.subtract).then_inc(var_ready, 1)
                invert(which)
                g, b = which[:3] + "_g" + which[3], which[:3] + "_b" + which[3]
                for s in range(KT + 3):
                    if s < KT:
                        if s < DVE_MOVES:
                            dve.wait_ge(recentred_dve, DVE_MOVES * i + s + 1)
                        else:
                            dve.wait_ge(recentred, (KT - DVE_MOVES) * i + s - DVE_MOVES + 1)
                        dve.tensor_tensor(dev[:, s, :], dev[:, s, :], spread_inverse, ALU.mult).then_inc(scaled, 1)
                    if 1 <= s <= KT and dve_affine(which, s - 1):
                        t = s - 1
                        dve.wait_ge(scaled, KT * i + t + 1)
                        dve.tensor_scalar(x[:, t, :], dev[:, t, :], col(g, t), col(b, t), ALU.mult, ALU.add).then_inc(normed_dve, 1)
                    if s >= 3 and not last:
                        low_part(which, s - 3, x)

            dve.memset(small[:, 92:93], RMS_EPS)
            dve.memset(small[:, 93:94], LN_EPS).then_inc(prep, 1)
            for t in range(1, KT, 2):
                dve.wait_ge(load_x[t // 2], 16)
                dve.tensor_tensor(dev[:, t, :], x[:, t, :], x[:, t, :], ALU.mult).then_inc(dve_squared, 1)
            dve.wait_ge(load_vec, 16)
            dve.wait_ge(load_ident, 16)
            lo_part(0)
            rms("mix", "norm_mix_g", dev)
            lo_part(1)
            lo_part(2)

            neg, z, z2, poly = (soft[:, i, :] for i in range(4))

            def step_prepare_scalars():
                for at, name, n in ((HBA, "rg_b_a", KT), (HBX, "rg_b_x", KT), (HBG, "b_gate", 3 * KT)):
                    dve.tensor_scalar(small[:, at:at + n], col(name, 0, n), 0.5, None, ALU.mult)
                dve.tensor_scalar(small[:, G08:G08 + 1], col("subln_g"), 1.0 - LAM_INIT, None, ALU.mult)
                for i in range(2):
                    link(dve.tensor_tensor_reduce(out=lamdot[:], in0=col(f"lq{i + 1}", 0, HD), in1=col(f"lk{i + 1}", 0, HD), scale=1.0,
                                                  scalar=0.0, op0=ALU.mult, op1=ALU.add, accum_out=small[:, LAMS + i:LAMS + i + 1]))
                link(dve.tensor_scalar(neg, col("rg_lambda", 0, KT), -1.0, None, ALU.mult))
                dve.tensor_tensor(small[:, SP2:SP2 + KT], neg, col("rg_lambda", 0, KT), ALU.max).then_inc(prep, 1)

            def step_prepare_turns():
                dve.wait_ge(load_pos, 16)
                dve.wait_ge(load_const, 16)
                link(dve.tensor_copy(tmp[:, 1, :], ipos[:]))
                link(dve.tensor_scalar(tmp[:, 0, :], tmp[:, 1, :], cst("freq", 1), None, ALU.mult))
                link(dve.tensor_scalar(tmp[:, 1, :], tmp[:, 0, :], 1.0 / (2 * math.pi), None, ALU.mult))
                link(dve.tensor_scalar(tmp[:, 1, :], tmp[:, 1, :], ROUND, None, ALU.add))
                link(dve.tensor_scalar(tmp[:, 1, :], tmp[:, 1, :], -ROUND, None, ALU.add))

            def step_prepare_angles():
                for part in TWO_PI:
                    link(dve.scalar_tensor_tensor(tmp[:, 0, :], tmp[:, 1, :], -part, tmp[:, 0, :], ALU.mult, ALU.add))
                dve.tensor_scalar(tmp[:, 0, :], tmp[:, 0, :], PI32, -PI32, ALU.min, ALU.max).then_inc(angles, 1)

            def step_prepare_series():
                dve.wait_ge(lam_exp, 2)
                y = small[:, SP2:SP2 + KT]
                link(dve.tensor_scalar(z, y, 2.0, None, ALU.add))
                link(dve.reciprocal(z, z))
                link(dve.tensor_tensor(z, z, y, ALU.mult))
                link(dve.tensor_tensor(z2, z, z, ALU.mult))
                link(dve.tensor_scalar(poly, z2, 1.0 / 15, 1.0 / 13, ALU.mult, ALU.add))
                terms(11)

            def terms(*ds):
                for d in ds:
                    link(dve.tensor_tensor(poly, poly, z2, ALU.mult))
                    link(dve.tensor_scalar(poly, poly, 1.0 / d, None, ALU.add))

            def step_prepare_sum():
                terms(9, 7, 5, 3)

            def step_prepare_softplus():
                terms(1)
                link(dve.tensor_tensor(poly, poly, z, ALU.mult))
                link(dve.tensor_scalar(neg, neg, 0.0, 2.0, ALU.max, ALU.mult))
                link(dve.scalar_tensor_tensor(small[:, SP2:SP2 + KT], poly, 4.0, neg, ALU.mult, ALU.add))
                link(dve.tensor_tensor(small[:, NLAM:NLAM + 1], small[:, LAMS + 3:LAMS + 4], small[:, LAMS + 2:LAMS + 3], ALU.subtract))
                link(dve.tensor_scalar(small[:, NLAM:NLAM + 1], small[:, NLAM:NLAM + 1], -LAM_INIT, None, ALU.add))

            def step_prepare_cosines():
                dve.wait_ge(sines, 2)
                link(dve.tensor_tensor(rope_cs[:, 0, :], rope_cs[:, 0, :], rope_cs[:, 0, :], ALU.mult))
                link(dve.tensor_scalar(rope_cs[:, 0, :], rope_cs[:, 0, :], -2.0, 1.0, ALU.mult, ALU.add))
                dve.memset(small[:, 91:92], 0.0).then_inc(prep, 1)

            def step_scores(j):
                s = j % 4
                dve.wait_ge(scored, j + 1)
                slope = head(j)[5]
                if slope is not None:
                    dve.wait_ge(tabled, j + 1)
                    tab = table[:, j % 2, :]
                else:
                    tab = cst("slide", 3 * P)
                if j >= 4:
                    dve.wait_ge(turned, weight_job(j - 4) + 1)
                neg_max = small[:, NEGM + 2 * s:NEGM + 2 * s + 2]
                for q, (a, b) in enumerate(((0, P), (P, 3 * P))):
                    r = dve.tensor_tensor_reduce(out=prob[:, s, a:b], in0=ps_score[:, a:b], in1=tab[:, a:b], scale=HD ** -0.5,
                                                 scalar=-3.0e38, op0=ALU.add, op1=ALU.max, accum_out=neg_max[:, q:q + 1])
                link(r)
                if slope is not None:
                    dve.tensor_scalar(neg_max, neg_max, -1.0, None, ALU.mult).then_inc(logits, 1)
                else:
                    dve.tensor_scalar(neg_max, neg_max, col(f"sinks{(j - 16) // 8}", (j - 16) % 8), -1.0, ALU.max, ALU.mult).then_inc(logits, 1)

            def step_weights(w):
                js = score_heads(w)
                dve.wait_ge(expd, js[-1] + 1)
                for j in js:
                    s = j % 4
                    total = small[:, ROWSUM + 2 * s:ROWSUM + 2 * s + 2]
                    if w >= 12:
                        link(dve.tensor_tensor(total, total, small[:, SINK + 2 * s:SINK + 2 * s + 2], ALU.add))
                    link(dve.reciprocal(small[:, RECIP + 2 * s:RECIP + 2 * s + 2], total))
                s = js[0] % 4
                ranges = ((0, 0, P), (1, P, 3 * P))
                if len(js) == 2:
                    s1 = js[1] % 4
                    r1 = small[:, RECIP + 2 * s1:RECIP + 2 * s1 + 2]
                    link(dve.tensor_scalar(r1, r1, small[:, NLAM:NLAM + 1], None, ALU.mult))
                for q, a, b in ranges:
                    r = dve.tensor_scalar(prob[:, s, a:b], prob[:, s, a:b], small[:, RECIP + 2 * s + q:RECIP + 2 * s + q + 1], None, ALU.mult)
                    if len(js) == 2:
                        link(r)
                        r = dve.scalar_tensor_tensor(prob[:, s, a:b], prob[:, s1, a:b], r1[:, q:q + 1], prob[:, s, a:b], ALU.mult, ALU.add)
                r.then_inc(weighted, 1)

            def step_values(w):
                if 8 <= w < 12 or w % 2 == 0:
                    return
                i = w // 2 if w < 8 else 4 + (w - 12) // 2
                y = w // 2 if w < 8 else 2 + ((w - 12) % 8) // 2
                dve.wait_ge(out_hi, i + 1)
                low(ylo[:, y, :], ps_out[:, 0:S], yhi[:, y, :], out_read)

            def step_diff_stats():
                dve.wait_ge(misc_read, MISC[("diff_stats",)] + 1)
                dve.wait_ge(diff_root, 1)
                link(dve.reciprocal(u1[:, VC:VC + 4, :], u1[:, VC:VC + 4, :]))

            def step_diff_norm():
                for h in range(DIFF_H):
                    o = u1[:, QC + h, :]
                    dve.scalar_tensor_tensor(o, o, small[:, G08:G08 + 1], u1[:, VC + h, :], ALU.mult, ALU.mult).then_inc(diff_y, 1)
                for h in range(DIFF_H):
                    dve.wait_ge(diff_hi, h + 1)
                    low(ylo[:, 12 + h, :], u1[:, QC + h, :], yhi[:, 12 + h, :], diff_lo)

            def step_rg_gates(t):
                dve.wait_ge(misc_read, MISC[("rg_gates", t)] + 1)
                xr = u1[:, XR + t, :]
                dve.scalar_tensor_tensor(xr, tmp[:, 2 + t % 2, :], 1.0, xr, ALU.add, ALU.mult).then_inc(rg_in, 1)

            def step_rg_recip(t):
                dve.wait_ge(rg_tanh, 2 * t + 2)
                rec = u1[:, KC + t, :]
                link(dve.tensor_scalar(rec, u1[:, QA + t, :], 1.0, None, ALU.add))
                dve.reciprocal(rec, rec).then_inc(rg_recip, 1)

            def step_rg_scan(t):
                dve.wait_ge(rg_driven, t + 1)
                dve.tensor_tensor_scan(u1[:, VA + t, :], u1[:, QA + t, :], u1[:, XR + t, :], 0.0, ALU.mult, ALU.add).then_inc(rg_state, 1)

            def step_rg_split(t):
                dve.wait_ge(rg_hi, t + 1)
                low(ylo[:, 4 + t, :], u1[:, XR + t, :], yhi[:, 4 + t, :], rg_lo)

            def step_rope(l, i):
                dve.wait_ge(misc_done, MISC[("rope", l, i)] + 1)
                t = u2[:, K2 if i == 0 else Q2 + i - 1, :]
                wait(dve, roped, 5 * l + i)
                dve.tensor_tensor(tmp[:, 3, :], ps_misc[:, 0:S], rope_cs[:, 1, :], ALU.mult).then_inc(misc_read, 1)
                link(dve.tensor_tensor(t, t, rope_cs[:, 0, :], ALU.mult))
                dve.wait_ge(misc_read, MISC[("rope", l, i)] + 1)
                dve.tensor_tensor(t, t, tmp[:, 3, :], ALU.add).then_inc(roped, 1)

            def step_pool_mix(l):
                dve.wait_ge(pool_hi, l + 1)
                dve.tensor_tensor(ylo[:, 0:2, :], u2[:, 39:41, :], yhi[:, 0:2, :].bitcast(f32), ALU.subtract).then_inc(pool_lo, 1)

            def step_gated_conv(l, t):
                dve.wait_ge(copied, copies_before(l) + 14)
                if t == 0:
                    link(dve.memset(zpad[:, :, 0:2], 0.0))
                y, z = u2[:, XC + t, :], zpad[:, t, :]
                link(dve.tensor_tensor(z[:, 2:], u2[:, GC + t, :], y, ALU.mult))
                link(dve.tensor_scalar(y, z[:, 2:], col(f"conv{l}", 3 * t + 2), None, ALU.mult))
                for k in (1, 0):
                    link(dve.scalar_tensor_tensor(y, z[:, k:k + S], col(f"conv{l}", 3 * t + k), y, ALU.mult, ALU.add))
                dve.tensor_tensor(y, y, u2[:, GB + t, :], ALU.mult).then_inc(gconv, 1)
                dve.wait_ge(gconv_hi, 2 * l + t + 1)
                low(ylo[:, 6 + t, :], y, yhi[:, 6 + t, :], gconv_lo)

            STEPS = {"prepare_scalars": step_prepare_scalars, "prepare_turns": step_prepare_turns,
                     "prepare_angles": step_prepare_angles, "prepare_series": step_prepare_series,
                     "prepare_sum": step_prepare_sum, "prepare_softplus": step_prepare_softplus,
                     "prepare_cosines": step_prepare_cosines, "scores": step_scores, "weights": step_weights, "values": step_values,
                     "diff_stats": step_diff_stats, "diff_norm": step_diff_norm, "rg_gates": step_rg_gates, "rg_recip": step_rg_recip, "rg_scan": step_rg_scan,
                     "rg_split": step_rg_split, "rope": step_rope, "pool_mix": step_pool_mix, "gated_conv": step_gated_conv}

            def steps(n, last):
                for name, *a in SLOTS.get(n + 1, []):
                    if name == "weights":
                        STEPS[name](*a)
                if n < last:
                    lo_part(n + 3)
                for name, *a in SLOTS.get(n, []):
                    if name in STEPS and name != "weights":
                        STEPS[name](*a)

            def merge(l, first, result, units, base):
                def split(t):
                    dve.wait_ge(m_hi, base + t + 1)
                    dve.scalar_tensor_tensor(xlo[:, t, :], merged_tile(base, t), 0.5, xhi[:, t, :].bitcast(f32), ALU.mult,
                                             ALU.subtract).then_inc(m_lo, 1)

                n, r = first, result
                for t in range(KT):
                    for unit, branches in enumerate(units):
                        lo_part(n + 2)
                        dve.wait_ge(unit_done, n + 1)
                        if t >= 2:
                            dve.wait_ge(merged, base + t - 1)
                            dve.wait_ge(m_lo, base + t - 1)
                        for which, branch in enumerate(branches):
                            ins = dve.scalar_tensor_tensor(branch_part(base, t, branch), gate_tile(l, branch, t), 1.0,
                                                           branch_bank(r, which, t), ALU.add, ALU.mult)
                        ins.then_inc(branch_read, 1)
                        n, r = n + 1, r + 1
                    if t:
                        split(t - 1)
                split(KT - 1)

            def residual(name, t, n, alpha, bank, it=0, per=0, tiles=0):
                wait(dve, unit_done, n + 1, it, per)
                dve.scalar_tensor_tensor(tile(x, t, it, tiles), tile(x, t, it, tiles), alpha, as_tile(bank[:, 0:S]), ALU.mult, ALU.add) \
                    .then_inc(res_new, 1)

            def wout(name, which, alpha):
                for t in range(KT):
                    lo_part(START[name] + t + 2)
                    if which in LNI and t >= 2:
                        for u in [0, 1] if t == 2 else [t - 1]:
                            deviation(which, u)
                    residual(name, t, START[name] + t, alpha, bank_of(RESULT[name] + t))
                if which in LNI:
                    deviation(which, KT - 1)

            def up(f, name, cols, width):
                def body(n, i, it):
                    lo_part(n + 2, it, 6)
                    q = KT + UPT * f + i
                    dst = (ugate, uval)[i % 2][:, (i // 2) % 3, :]
                    ps = bank_of(RESULT[name] + i)
                    wait(dve, conv_start, q + 1, it, 6)
                    dve.scalar_tensor_tensor(dst[:, 1:], ps[:, 0:S - 1], tap(cols, width, 1, i, it), dst[:, 1:], ALU.mult, ALU.add) \
                        .then_inc(tap1, 1)
                    wait(dve, tap1, q - KT + 1, it, 6)
                    dve.scalar_tensor_tensor(dst[:, 2:], ps[:, 0:S - 2], tap(cols, width, 0, i, it), dst[:, 2:], ALU.mult, ALU.add) \
                        .then_inc(conv_done, 1)
                repeat(dve, name, UPT, 6, body, peel_first=True)

            def down(name, which, alpha):
                def body(n, i, it):
                    lo_part(n + 2, it, 6)
                    t = i // 3
                    if which in LNI and i % 3 == 0 and not (isinstance(it, int) and t < 2):
                        deviation(which, t - 2, it)
                    if i % 3 == 2:
                        if which in LNI and t == KT - 1:
                            deviation(which, KT - 2)
                        residual(name, t, n, alpha, down_bank(name, t), it, 6, 2)
                repeat(dve, name, DOWN, 6, body, peel_first=True)
                if which in LNI:
                    deviation(which, KT - 1)

            for n in range(WIN1):
                if 24 <= n < 32:
                    t = n - 24
                    ps, xr = bank_of(n), u1[:, XR + t, :]
                    dve.wait_ge(conv_start, t + 1)
                    for back in (1, 2):
                        link(dve.scalar_tensor_tensor(xr[:, back:], ps[:, 0:S - back], col("rg_conv", 5 * t + 3 - back), xr[:, back:],
                                                      ALU.mult, ALU.add))
                    dve.scalar_tensor_tensor(xr[:, 3:], ps[:, 0:S - 3], col("rg_conv", 5 * t), xr[:, 3:], ALU.mult, ALU.add) \
                        .then_inc(conv_done, 1)
                steps(n, WIN1 - 1)
            merge(None, START["merge1"], RESULT["merge1"], [(0, 2), (1,)], 0)
            wout("wout1", "ffn", 1.0)
            rms("ffn", "norm_ffn_g", dev)
            up(0, "up1", "ffn_1", 4)
            down("down1", "final", 1.0)
            rms("final", "final_g", x)
            for l in range(LAYERS2):
                lo_part(START[f"win2{l}"] + 2)
                for n in range(START[f"win2{l}"], START[f"merge2{l}"]):
                    steps(n, START[f"merge2{l}"] - 1)
                merge(l, START[f"merge2{l}"], RESULT[f"merge2{l}"], [(0, 1, 2)], KT * (1 + l))
                wout(f"wout2{l}", f"ln1{l}", ALPHA)
                layer_norm(f"ln1{l}", False)
                up(1 + l, f"up2{l}", f"ffn_2{l}", 3)
                down(f"down2{l}", f"ln2{l}", ALPHA)
                layer_norm(f"ln2{l}", l == LAYERS2 - 1)


ROUND = 1.5 * 2.0 ** 23


def _two_pi_parts():
    parts, rest = [], 2 * math.pi
    for _ in range(4):
        e = math.floor(math.log2(rest)) - 9
        p = math.floor(rest / 2.0 ** e) * 2.0 ** e
        parts.append(p)
        rest -= p
    return parts


TWO_PI = _two_pi_parts()
PI32 = 3.1415925


def _tiles(w):
    k, n = w.shape
    return np.ascontiguousarray(w.reshape(k // P, P, n // P, P).transpose(2, 1, 0, 3).reshape(n // P, P, k))


def _cols(v):
    return v.reshape(-1, P).T


def _block_diagonal(w):
    t = w.shape[0] // 2
    out = np.zeros((P, t, P), w.dtype)
    for i in range(2 * t):
        h = 64 * (i % 2)
        out[h:h + 64, i // 2, h:h + 64] = w[i]
    return out


def _interleave(a):
    s = a.shape[:-1]
    return a.reshape(*s, 2, FT, P).swapaxes(-3, -2).reshape(*s, 2 * FF)


def _heads_in_pairs(a):
    s = a.shape[:-1]
    return a.reshape(*s, 2, 4, HD).swapaxes(-3, -2).reshape(*s, 8 * HD)


def layout(g):
    out = {"x": np.ascontiguousarray(g["x"][0].T.reshape(KT, P, S).transpose(1, 0, 2)), "const": constants()}
    w = {"w_win1": _tiles(g["w_in"][0])}
    a, b, c = (_tiles(g[f"w_branch_{n}"][0]) for n in "abc")
    w["w_merge1"] = np.concatenate([a, c, b], 2)
    w["w_out1"] = _tiles(g["w_out"][0])
    w["w_up1"] = _tiles(_interleave(g["ffn_up"][0]))
    w["w_down1"] = _tiles(g["ffn_down"][0])
    vec = np.zeros((P, NCOLS), np.float32)

    def put(name, cols):
        vec[:, COLS[name]:COLS[name] + cols.shape[1]] = cols

    def by_tile(rows):
        return np.stack([_cols(r) for r in rows], 2).reshape(P, -1)

    put("norm_mix_g", _cols(g["norm_mix_g"][0]))
    put("b_gate", _cols(g["b_gate"][0]))
    put("rg_conv", by_tile([*g["rg_conv_w"][0], g["rg_conv_b"][0]]))
    for name in ("rg_b_a", "rg_b_x", "rg_lambda", "norm_ffn_g"):
        put(name, _cols(g[name][0]))
    put("subln_g", _cols(g["diff_subln_g"][0]))
    put("final_g", _cols(g["final_norm_g"]))
    put("ffn_1", by_tile([_interleave(r) for r in (*g["ffn_conv_w"][0], g["ffn_conv_b"][0])]))
    for i in (1, 2):
        for n in "qk":
            put(f"l{n}{i}", np.broadcast_to(g[f"diff_l{n}{i}"][0], (P, HD)))
    out["rg_w"] = np.concatenate([_block_diagonal(g["rg_w_a"][0]), _block_diagonal(g["rg_w_x"][0])], 1)
    pool = []
    for l in range(LAYERS2):
        w_in = g["w_in_2"][l]
        u, q, k, v, xc, gb, gc, gates = np.split(w_in, np.cumsum([256, 512, 128, 128, 256, 256, 256]), 1)
        w[f"w_win2{l}"] = _tiles(np.concatenate([k, v, _heads_in_pairs(q), u, xc, gb, gc, gates], 1))
        a, b, c = g["w_branch_a_2"][l], g["w_branch_b_2"][l], g["w_branch_c_2"][l]
        w[f"w_merge2{l}"] = np.concatenate([_tiles(a), _tiles(_heads_in_pairs(b.T).T), _tiles(c)], 2)
        w[f"w_out2{l}"] = _tiles(g["w_o_2"][l])
        w[f"w_up2{l}"] = _tiles(_interleave(g["w_up_2"][l]))
        w[f"w_down2{l}"] = _tiles(g["w_down_2"][l])
        put(f"pool_scale{l}", _cols(g["pool_scale_2"][l]))
        put(f"conv{l}", by_tile(list(g["conv_w_2"][l])))
        put(f"ffn_2{l}", by_tile([_interleave(r) for r in g["ffn_conv_w_2"][l]]))
        for name in ("ln1_g", "ln1_b", "ln2_g", "ln2_b"):
            put(f"{name}{l}", _cols(g[f"{name}_2"][l]))
        put(f"sinks{l}", np.broadcast_to(g["attn_sinks_2"][l].reshape(2, 4).T.reshape(8), (P, 8)))
        pool.append(_block_diagonal(g["w_pool_2"][l]))
    out["pool_w"] = np.concatenate(pool, 1)
    out["positions"] = np.ascontiguousarray(np.broadcast_to(g["positions_2"], (P, S)))
    return {**out, "vec": vec, **w}


def kernel(**inputs):
    import concourse.bacc as bacc
    from concourse.bass_utils import run_bass_kernel_spmd

    arrays = layout({k: np.asarray(v) for k, v in inputs.items()})
    nc = bacc.Bacc("TRN2", target_bir_lowering=False, num_devices=1)
    args = {n: nc.dram_tensor(f"in_{n}", a.shape, mybir.dt.from_np(a.dtype), kind="ExternalInput").ap() for n, a in arrays.items()}
    out = nc.dram_tensor("out_x", (P, KT, S), mybir.dt.float32, kind="ExternalOutput").ap()
    build(nc, args, out)
    r = run_bass_kernel_spmd(nc, [{f"in_{n}": a for n, a in arrays.items()}], core_ids=[0])
    return np.ascontiguousarray(r.results[0]["out_x"].transpose(2, 1, 0).reshape(1, S, DM))
```
